# Optimizing a Trainium2 kernel written in Bass

```python
import jax, jax.numpy as jnp
from jax import lax
import numpy as np

D_MODEL = 2048
BATCH = 1
SEQ = 512
DEPTH = 1
DEC_BATCH = 8
DEC_SEQ = 1
PAST_LEN = 4096
PAGE_SIZE = 128

D_MIX = D_MODEL
D_RET = D_MIX // 2
D_ATT = D_MIX - D_RET
HEAD_DIM = 128
N_RET_HEADS = D_RET // HEAD_DIM
N_ATT_HEADS = D_ATT // HEAD_DIM
N_KV_HEADS = 2
N_GROUP = N_ATT_HEADS // N_KV_HEADS
D_KV = N_KV_HEADS * HEAD_DIM
N_IDX_HEADS = 16
D_IDX = 128
TOPK_MAX = 256
RET_CHUNK = 128
Q_BLOCK = 128
ROPE_BASE = 10000.0
NORM_EPS = 1e-6
SPLITS = (D_RET, D_RET, D_RET, D_RET, D_ATT, D_KV, D_KV, D_ATT, N_IDX_HEADS * D_IDX, D_IDX, N_IDX_HEADS)
D_IN_PROJ = 4 * D_RET + 2 * D_ATT + 2 * D_KV + N_IDX_HEADS * D_IDX + D_IDX + N_IDX_HEADS

kernel_name = "hymba_retention_dsa_step"

def rmsnorm(x, g):
    xf = x.astype(jnp.float32)
    y = xf * lax.rsqrt(jnp.mean(xf * xf, -1, keepdims=True) + NORM_EPS)
    return (y * g.astype(jnp.float32)).astype(x.dtype)

def head_group_norm(o, g):
    of = o.astype(jnp.float32)
    mu = jnp.mean(of, -1, keepdims=True)
    var = jnp.mean(jnp.square(of - mu), -1, keepdims=True)
    return ((of - mu) * lax.rsqrt(var + NORM_EPS) * g.astype(jnp.float32)).astype(o.dtype)

def rotary(x, pos):
    half = x.shape[-1] // 2
    inv = ROPE_BASE ** (-jnp.arange(half, dtype=jnp.float32) / half)
    ang = pos.astype(jnp.float32)[:, None] * inv[None, :]
    cos = jnp.cos(ang)[None, :, None, :].astype(x.dtype)
    sin = jnp.sin(ang)[None, :, None, :].astype(x.dtype)
    x1, x2 = x[..., :half], x[..., half:]
    return jnp.concatenate([x1 * cos - x2 * sin, x1 * sin + x2 * cos], -1)

def retention_log_decay():
    return jnp.log1p(-jnp.exp2(-5.0 - jnp.arange(N_RET_HEADS, dtype=jnp.float32)))

def retention_chunk(q, k, v, s_prev, log_g):
    c = q.shape[1]
    i = jnp.arange(c, dtype=jnp.float32)
    diff = i[:, None] - i[None, :]
    decay = jnp.where(diff[None] >= 0, jnp.exp(jnp.maximum(diff, 0.0)[None] * log_g[:, None, None]), 0.0).astype(q.dtype)
    scores = jnp.einsum('bihd,bjhd->bhij', q, k) * decay[None]
    inner = jnp.einsum('bhij,bjhe->bihe', scores, v)
    q_dec = jnp.exp((i[:, None] + 1.0) * log_g[None, :]).astype(q.dtype)
    cross = jnp.einsum('bihd,bhde->bihe', q, s_prev.astype(q.dtype)) * q_dec[None, :, :, None]
    k_dec = jnp.exp((c - 1.0 - i)[:, None] * log_g[None, :]).astype(k.dtype)
    s_new = jnp.exp(c * log_g).astype(s_prev.dtype)[None, :, None, None] * s_prev + jnp.einsum('bjhd,bjhe->bhde', k * k_dec[None, :, :, None], v)
    return inner + cross, s_new.astype(s_prev.dtype)

def retention_prompt(q, k, v, log_g):
    b, t, h, d = q.shape
    c = min(RET_CHUNK, t)
    nc = t // c
    def chunks(a):
        return jnp.moveaxis(a.reshape((b, nc, c) + a.shape[2:]), 1, 0)
    s0 = jnp.zeros((b, h, d, v.shape[-1]), dtype=v.dtype)
    def step(s, qkv):
        o, s = retention_chunk(qkv[0], qkv[1], qkv[2], s, log_g)
        return s, o
    s_fin, outs = lax.scan(step, s0, (chunks(q), chunks(k), chunks(v)))
    return jnp.moveaxis(outs, 0, 1).reshape(b, t, h, v.shape[-1]), s_fin

def project(x, g_norm, w_in, pos):
    b, t = x.shape[:2]
    z = rmsnorm(x, g_norm) @ w_in
    offs = [int(o) for o in np.cumsum(SPLITS)[:-1]]
    q_r, k_r, v_r, g_r, q_a, k_a, v_a, g_a, q_i, k_i, w_i = jnp.split(z, offs, axis=-1)
    q_r = rotary(q_r.reshape(b, t, N_RET_HEADS, HEAD_DIM), pos)
    k_r = rotary(k_r.reshape(b, t, N_RET_HEADS, HEAD_DIM), pos) * (HEAD_DIM ** -0.5)
    v_r = v_r.reshape(b, t, N_RET_HEADS, HEAD_DIM)
    q_a = q_a.reshape(b, t, N_KV_HEADS, N_GROUP, HEAD_DIM)
    k_a = k_a.reshape(b, t, N_KV_HEADS, HEAD_DIM)
    v_a = v_a.reshape(b, t, N_KV_HEADS, HEAD_DIM)
    q_i = q_i.reshape(b, t, N_IDX_HEADS, D_IDX)
    w_i = w_i * (N_IDX_HEADS ** -0.5 * D_IDX ** -0.5)
    return q_r, k_r, v_r, g_r, q_a, k_a, v_a, g_a, q_i, k_i, w_i

def indexer_select(q_i, w_i, k_i_all, q_pos, n_sel):
    rel = jax.nn.relu(jnp.einsum('bqhd,bsd->bqhs', q_i, k_i_all))
    score = jnp.einsum('bqh,bqhs->bqs', w_i, rel).astype(jnp.float32)
    key_pos = jnp.arange(k_i_all.shape[1], dtype=jnp.int32)
    score = jnp.where(key_pos[None, None, :] <= q_pos[None, :, None], score, -jnp.inf)
    _, idx = lax.top_k(score, n_sel)
    valid = idx <= q_pos[None, :, None]
    return idx, valid

def sparse_attend(q, k_g, v_g, valid):
    b, nq = q.shape[:2]
    logits = jnp.einsum('bqcgd,bqkcd->bqcgk', q, k_g).astype(jnp.float32) * (HEAD_DIM ** -0.5)
    logits = jnp.where(valid[:, :, None, None, :], logits, -jnp.inf)
    p = jax.nn.softmax(logits, axis=-1).astype(v_g.dtype)
    o = jnp.einsum('bqcgk,bqkcd->bqcgd', p, v_g)
    return o.reshape(b, nq, D_ATT)

def dsa_prompt(q_a, k_a, v_a, q_i, k_i, w_i):
    b, t = q_a.shape[:2]
    n_sel = min(TOPK_MAX, t // 4)
    qb = min(Q_BLOCK, t)
    nb = t // qb
    def blocks(a):
        return jnp.moveaxis(a.reshape((b, nb, qb) + a.shape[2:]), 1, 0)
    starts = jnp.arange(nb, dtype=jnp.int32) * qb
    gather_rows = jax.vmap(lambda rows, ids: rows[ids])
    def one_block(args):
        qa, qi, wi, st = args
        q_pos = st + jnp.arange(qb, dtype=jnp.int32)
        idx, valid = indexer_select(qi, wi, k_i, q_pos, n_sel)
        return sparse_attend(qa, gather_rows(k_a, idx), gather_rows(v_a, idx), valid)
    out = lax.map(one_block, (blocks(q_a), blocks(q_i), blocks(w_i), starts))
    return jnp.moveaxis(out, 0, 1).reshape(b, t, D_ATT)

def dsa_sample(q_a, k_a, v_a, q_i, k_i, w_i, pool_k, pool_v, pool_ki, page_table):
    db, ds = q_a.shape[:2]
    page = pool_k.shape[1]
    past = page_table.shape[1] * page
    n_sel = min(TOPK_MAX, (past + ds) // 4)
    ki_past = pool_ki[page_table].reshape(db, past, D_IDX)
    ki_all = jnp.concatenate([ki_past.astype(k_i.dtype), k_i], axis=1)
    q_pos = past + jnp.arange(ds, dtype=jnp.int32)
    idx, valid = indexer_select(q_i, w_i, ki_all, q_pos, n_sel)
    b_ix = jnp.arange(db)[:, None, None]
    in_past = (idx < past)[..., None, None]
    pidx = jnp.minimum(idx, past - 1)
    phys = page_table[b_ix, pidx // page]
    off = pidx % page
    nidx = jnp.clip(idx - past, 0, ds - 1)
    k_g = jnp.where(in_past, pool_k[phys, off].astype(k_a.dtype), k_a[b_ix, nidx])
    v_g = jnp.where(in_past, pool_v[phys, off].astype(v_a.dtype), v_a[b_ix, nidx])
    return sparse_attend(q_a, k_g, v_g, valid)

def merge_heads(o_r, g_r, o_a, g_a, ret_g, w_out):
    b, t = o_r.shape[:2]
    r = head_group_norm(o_r, ret_g).reshape(b, t, D_RET) * jax.nn.silu(g_r)
    a = o_a * jax.nn.silu(g_a)
    return jnp.concatenate([r, a], axis=-1) @ w_out

def setup_inputs(seed: int = 0) -> dict:
    key = jax.random.key(seed)
    ks = jax.random.split(key, 12)
    n_pages = PAST_LEN // PAGE_SIZE
    n_used = DEC_BATCH * n_pages
    n_phys = n_used + (n_used + 3) // 4
    f32 = jnp.float32
    x_prompt = jax.random.normal(ks[0], (BATCH, SEQ, D_MODEL), f32)
    x_sample = jax.random.normal(ks[1], (DEC_BATCH, DEC_SEQ, D_MODEL), f32)
    cache_k = jax.random.normal(ks[2], (DEPTH, n_phys, PAGE_SIZE, N_KV_HEADS, HEAD_DIM), f32)
    cache_v = jax.random.normal(ks[3], (DEPTH, n_phys, PAGE_SIZE, N_KV_HEADS, HEAD_DIM), f32)
    cache_kidx = jax.random.normal(ks[4], (DEPTH, n_phys, PAGE_SIZE, D_IDX), f32)
    state_ret = jax.random.normal(ks[5], (DEPTH, DEC_BATCH, N_RET_HEADS, HEAD_DIM, HEAD_DIM), f32)
    page_table = jax.random.permutation(ks[6], n_phys)[:n_used].reshape(DEC_BATCH, n_pages).astype(jnp.int32)
    norm_g = 1.0 + 0.02 * jax.random.normal(ks[7], (DEPTH, D_MODEL), f32)
    w_in = jax.random.normal(ks[8], (DEPTH, D_MODEL, D_IN_PROJ), f32) * (D_MODEL ** -0.5)
    ret_norm_g = 1.0 + 0.02 * jax.random.normal(ks[9], (DEPTH, N_RET_HEADS, HEAD_DIM), f32)
    w_out = jax.random.normal(ks[10], (DEPTH, D_MIX, D_MODEL), f32) * (D_MIX ** -0.5)
    final_norm_g = 1.0 + 0.02 * jax.random.normal(ks[11], (D_MODEL,), f32)
    return {"x_prompt": x_prompt, "x_sample": x_sample, "cache_k": cache_k, "cache_v": cache_v,
            "cache_kidx": cache_kidx, "state_ret": state_ret, "page_table": page_table,
            "norm_g": norm_g, "w_in": w_in, "ret_norm_g": ret_norm_g, "w_out": w_out,
            "final_norm_g": final_norm_g}

def reference(x_prompt, x_sample, cache_k, cache_v, cache_kidx, state_ret, page_table,
              norm_g, w_in, ret_norm_g, w_out, final_norm_g):
    log_g = retention_log_decay()
    t = x_prompt.shape[1]
    ds = x_sample.shape[1]
    past = page_table.shape[1] * cache_k.shape[2]
    pos_p = jnp.arange(t, dtype=jnp.int32)
    pos_s = past + jnp.arange(ds, dtype=jnp.int32)
    hp, hs = x_prompt, x_sample
    pk, pv, pki, pst = [], [], [], []
    sk, sv, ski, sst = [], [], [], []
    for l in range(DEPTH):
        q_r, k_r, v_r, g_r, q_a, k_a, v_a, g_a, q_i, k_i, w_i = project(hp, norm_g[l], w_in[l], pos_p)
        o_r, s_fin = retention_prompt(q_r, k_r, v_r, log_g)
        o_a = dsa_prompt(q_a, k_a, v_a, q_i, k_i, w_i)
        hp = hp + merge_heads(o_r, g_r, o_a, g_a, ret_norm_g[l], w_out[l])
        pk.append(k_a); pv.append(v_a); pki.append(k_i); pst.append(s_fin)
        q_r, k_r, v_r, g_r, q_a, k_a, v_a, g_a, q_i, k_i, w_i = project(hs, norm_g[l], w_in[l], pos_s)
        o_r, s_new = retention_chunk(q_r, k_r, v_r, state_ret[l], log_g)
        o_a = dsa_sample(q_a, k_a, v_a, q_i, k_i, w_i, cache_k[l], cache_v[l], cache_kidx[l], page_table)
        hs = hs + merge_heads(o_r, g_r, o_a, g_a, ret_norm_g[l], w_out[l])
        sk.append(k_a); sv.append(v_a); ski.append(k_i); sst.append(s_new)
    y_prompt = rmsnorm(hp, final_norm_g)
    y_sample = rmsnorm(hs, final_norm_g)
    return (y_prompt, y_sample, jnp.stack(pk), jnp.stack(pv), jnp.stack(pki), jnp.stack(pst),
            jnp.stack(sk), jnp.stack(sv), jnp.stack(ski), jnp.stack(sst))


_drawn_inputs = setup_inputs


def setup_inputs(seed=0):
    import zlib

    import numpy as np

    out = dict(_drawn_inputs(seed))
    spreads = {}
    factors = {}
    for name, (base, spread) in spreads.items():
        noise = np.random.default_rng([zlib.crc32(name.encode()), seed]).standard_normal(out[name].shape)
        drawn = base * np.exp(spread * noise) if base else spread * noise
        out[name] = __import__('jax').numpy.asarray(drawn.astype(out[name].dtype))
    for name, factor in factors.items():
        out[name] = (out[name] * factor).astype(out[name].dtype)
    return out
```

```python
import concourse.bass as bass
from concourse import mybir
from concourse.alu_op_type import AluOpType as ALU
from contextlib import ExitStack

F32 = mybir.dt.float32
F32R = mybir.dt.float32r
I32 = mybir.dt.int32
U32 = mybir.dt.uint32
ACT = mybir.ActivationFunctionType
AXX = mybir.AxisListType.X

P = 128
DM = 2048
T = 512
NS = 8
NT = T + NS
HALF = NT // 2
KT = DM // P
KC = KT // 2
NH = 8
NKV = 2
NG = NH // NKV
NIH = 16
PAGES = 32
PAST = PAGES * P
NKEY = PAST + 1
SELP = 128
SELS = 256
EPS = 1e-6
NEG = -1e30
TAKEN = -3e38
SCALE = P ** -0.5
NB_IN, NB = 35, 43
QT = T // P
SEG = {2: 0, 0: 384, 1: 512, 3: 768}
SEGW = 1280


def build(nc, x_prompt, x_sample, cache_k, cache_v, cache_kidx, state_ret, page_table, norm_g, w_in,
          ret_norm_g, w_out, final_norm_g, c_ident, c_rot, c_tri, c_bias, c_cols, c_eye, c_iota,
          y_prompt, y_sample, nk_p, nv_p, nki_p, st_p, nk_s, nv_s, nki_s, st_s):
    ctx = ExitStack()
    with ctx:
        def sb(name, shape, dt=F32):
            return ctx.enter_context(nc.sbuf_tensor(name, shape, dt))

        def sem(name):
            return ctx.enter_context(nc.semaphore(name))

        Hh = sb("Hh", [P, KT, NT], F32R)
        Hl = sb("Hl", [P, KT, NT], F32R)
        Wraw = sb("Wraw", [P, 2, KC, 256])
        Wh = sb("Wh", [P, 2, KC, 256], F32R)
        Wl = sb("Wl", [P, 2, KC, 256], F32R)
        mix = sb("mix", [P, KT, NT])
        ident = sb("ident", [P, P])
        rot = sb("rot", [P, 2, NT])
        tri = sb("tri", [P, P])
        cols = sb("cols", [P, 6, NH])
        ctri = sb("ctri", [P, P])
        eye = sb("eye", [NS, NS])
        iota = sb("iota", [P, PAGES])
        gin = sb("gin", [P, KT])
        gret = sb("gret", [P, NH])
        ptb = sb("ptb", [P, NS, PAGES], I32)
        QB = sb("QB", [P, 16 * 68])
        st4 = sb("st4", [P, 64])
        rsq = sb("rsq", [P, 2, 4])
        bnst = sb("bnst", [P, 4, 6])
        mv = sb("mv", [P, 4, 2])
        idxu = sb("idxu", [NS, SELS], U32)
        top8 = sb("top8", [P, 8])
        OS = sb("OS", [P, NH, NS])

        base = nc.sbuf_base
        base = (base + 31) // 32 * 32
        room = nc.sbuf_usable_end - 32 - base
        at = {}

        def place(name, shape, dt, off):
            n = 4
            for s in shape[1:]:
                n *= s
            assert off + n <= room, (name, off, n, room)
            at[name] = (off, n)
            return nc.alloc_sbuf_tensor_at(name, shape, dt, offset=base + off), off + n

        XT, o = place("XT", [P, 2, DM], F32, 0)
        HT, o = place("HT", [P, 2, 4, P], F32, o)
        junk, _ = place("junk", [P, DM], F32, o)
        scores, o = place("scores", [NS, NKEY + 7], F32, 0)
        persist = o
        bm, o = place("bm", [P, SEGW], F32, persist)
        after_bm = o
        kiT, o = place("kiT", [P, NT], F32, o)
        wiT, o = place("wiT", [P, NT], F32, o)
        wn, o = place("wn", [P, 5, NIH], F32, o)
        kin, _ = place("kin", [P, 5, P], F32, o)
        relu, o2 = place("relu", [P, 2, T], F32, o)
        QS, _ = place("QS", [P, NS * 144], F32, o2)
        wsT, o3 = place("wsT", [NS, NS, NIH], F32, o2 + 4 * NS * 144)
        wsel, o3 = place("wsel", [P, NS], F32, o3)
        pidx, o3 = place("pidx", [P, NS, NS], U32, o3)
        pidf, o3 = place("pidf", [P, NS, NS], F32, o3)
        ptq, o3 = place("ptq", [P, NS, NS], I32, o3)
        kx, o3 = place("kx", [P, 4, 4 * P], F32, o3)
        kaT, o = place("kaT", [P, NKV, NT], F32, after_bm)
        vaT, o = place("vaT", [P, NKV, NT], F32, o)
        kan, o = place("kan", [P, 5, NKV * P], F32, o)
        van, o = place("van", [P, 5, NKV * P], F32, o)
        pb, o = place("pb", [P, SEGW], F32, o)
        pT, o = place("pT", [P, SEGW], F32, o)
        XS, o = place("XS", [P, 2, NT], F32, persist)
        XW, o = place("XW", [P, 2, NT], F32, o)
        kq, o = place("kq", [P, 2, NT], F32, o)
        vT, o = place("vT", [P, NT], F32, o)
        kn, o = place("kn", [P, 4, P], F32, o)
        vn, o = place("vn", [P, 4, P], F32, o)
        am, o = place("am", [P, 4, P], F32, o)
        nrm, o = place("nrm", [P, 4, P], F32, o)
        stt, o = place("stt", [P, 4, P], F32, o)
        sp_, o = place("sp_", [P, NS, P], F32, o)
        kns, o = place("kns", [NS, P], F32, o)
        vx, o = place("vx", [NS, NS, P], F32, o)
        kg, o = place("kg", [P, 2 * NS, 256], F32, 0)
        vg, o = place("vg", [P, 2 * NS, 256], F32, o)
        nkb, o = place("nkb", [P, NS, 256], F32, o)
        posf, o = place("posf", [P, 2, NS], F32, o)
        sidf, o = place("sidf", [NS, SELS], F32, o)
        posi, o = place("posi", [P, 4, 2 * NS], I32, o)
        posw, o = place("posw", [P, 2, 2 * NS], F32, o)
        rowu, o = place("rowu", [P, 2 * NS], U32, o)
        ohot, o = place("ohot", [P, 2 * NS, PAGES], F32, o)
        skT, o = place("skT", [P, 2, 512], F32, o)
        sprob, o = place("sprob", [64, SELS], F32, o)
        spT, o = place("spT", [P, P], F32, o)
        Y, o = place("Y", [P, QT, DM], F32, 0)
        Ys, o = place("Ys", [NS, DM], F32, o)
        gfb, o = place("gfb", [P, DM], F32, o)
        yT = mix[:, 0:2, :]

        bank = [ctx.enter_context(nc.psum_tensor(f"bank{i}", [P, 512], F32)) for i in range(8)]

        s_const = sem("s_const"); s_ident = sem("s_ident"); s_gin = sem("s_gin"); s_ptab = sem("s_ptab")
        x_in = [sem("x_in0"), sem("x_in1")]
        x_sq = sem("x_sq"); x_norm = sem("x_norm"); x_tr = sem("x_tr"); x_g = sem("x_g")
        h_hi = sem("h_hi"); h_lo = sem("h_lo")
        w_in_sem = [sem("w_landed0"), sem("w_landed1")]
        w_hi = sem("w_hi"); w_lo = sem("w_lo"); a_used = sem("chunk_a_used")
        acc_done = sem("acc_done"); acc_free = sem("acc_free")
        dch = sem("dve_chain"); ach = sem("act_chain"); pch = sem("pool_chain")
        st_out = sem("stores_done")
        ki_tr = sem("ki_tr"); ki_ev = sem("ki_ev")
        si_mm = sem("si_mm"); si_relu = sem("si_relu"); si_acc = sem("si_acc")
        ws_ready = sem("ws_ready"); ws_tr = sem("ws_tr"); wsel_ready = sem("wsel_ready"); qs_ready = sem("qs_ready")
        pidx_ready = sem("pidx_ready"); kx_in = [sem(f"kx_in{i}") for i in range(4)]
        kx_tr = sem("kx_tr"); kt_ev = sem("kt_ev"); kt_used = sem("kt_used")
        sc_relu = sem("sc_relu"); sc_row = sem("sc_row"); sc_out = sem("sc_out"); bm_ready = sem("bm_ready")
        kv_tr = sem("kv_tr"); kv_ev = sem("kv_ev"); qb_ready = sem("qb_ready")
        al_mm = sem("al_mm"); al_bias = sem("al_bias"); al_max = sem("al_max"); al_exp = sem("al_exp")
        p_ready = sem("p_ready"); at_tr = sem("at_tr"); at_ev = sem("at_ev"); av_mm = sem("av_mm"); av_mix = sem("av_mix")
        xs_ev = sem("xs_ev"); rot_done = sem("rot_done")
        kn_tr = sem("kn_tr"); kn_ev = sem("kn_ev"); sT_mm = sem("sT_mm"); am_ready = sem("am_ready")
        vn_tr = sem("vn_tr"); vn_ev = sem("vn_ev"); vx_ready = sem("vx_ready"); u_mm = sem("u_mm"); s_ready = sem("s_ready")
        us_mm = sem("us_mm"); sn_ready = sem("sn_ready"); sp_in = sem("sp_in"); ro_mm = sem("ro_mm"); ro_stat = sem("ro_stat")
        ro_nrm = sem("ro_nrm"); os_ev = sem("os_ev"); rn_tr = sem("rn_tr"); rn_mix = sem("rn_mix"); ros_mm = sem("ros_mm")
        st_s_out = sem("st_s_out"); st_p_out = sem("st_p_out")
        gs_tr = sem("gs_tr"); gs_n = sem("gs_n")
        sel_f = sem("sel_f"); sel_tr = sem("sel_tr"); row_ready = sem("row_ready"); nkb_in = sem("nkb_in")
        kg_in = [sem(f"kg_in{i}") for i in range(2 * NS)]
        vg_in = [sem(f"vg_in{i}") for i in range(2 * NS)]
        kg_fix = sem("kg_fix"); vg_fix = sem("vg_fix"); sk_tr = sem("sk_tr"); sk_ev = sem("sk_ev"); sl_mm = sem("sl_mm")
        sl_max = sem("sl_max"); sl_exp = sem("sl_exp"); sp_ready = sem("sp_ready"); spt_tr = sem("spt_tr"); spt_ev = sem("spt_ev")
        so_mm = sem("so_mm"); mix_ready = sem("mix_ready"); m_hi = sem("m_hi"); m_lo = sem("m_lo")
        y_res = sem("y_res"); y_tr = sem("y_tr"); y_add = sem("y_add"); y_sq = sem("y_sq"); y_norm = sem("y_norm")

        wiv = w_in[0].rearrange("(k p) c -> p k c", p=P)
        wov = w_out[0].rearrange("(k p) c -> p k c", p=P)

        def pieces(n):
            if n == 0:
                return [(0, 8704, 144)]
            if n <= 8:
                return [(0, 6656 + 256 * (n - 1), 256)]
            if n <= 10:
                return [(0, 5120 + 256 * (n - 9), 256)]
            if n <= 18:
                j = (n - 11) // 2
                return [(0, (4096 if n % 2 else 5632) + 256 * j, 256)]
            if n < NB_IN:
                h = (n - 19) // 2
                a, b = (1024, 0) if n % 2 else (2048, 3072)
                return [(0, a + P * h, P), (P, b + P * h, P)]
            return [(0, 256 * (n - NB_IN), 256)]

        def landed(n):
            return 16 * sum(len(pieces(i)) for i in range(n + 1))

        def width(n):
            return 144 if n == 0 else 256

        def tile_cols(n, t):
            return slice(16, 144) if n == 0 and t else slice(P * t, P * t + P)

        def tok(i):
            return slice(P * i, P * i + P) if i < QT else slice(T, NT)

        def rows(i):
            return P if i < QT else NS

        block = ctx.enter_context(nc.Block())

        @block.sync
        def _(sp):
            stores = [0]

            def store(dst, src, s=None):
                sp.dma_start(dst, src).then_inc(s or st_out, 16)
                if s is None:
                    stores[0] += 16

            def weights(n, a):
                if n >= 1:
                    sp.wait_ge(w_lo, 2 * (n - 1) + a + 1)
                src = wiv if n < NB_IN else wov
                for dst, c, m in pieces(n):
                    sp.dma_start(Wraw[:, a, :, dst:dst + m],
                                 src[:, KC * a:KC * a + KC, c:c + m]).then_inc(w_in_sem[a], 16)

            sp.dma_start(ident[:, :], c_ident).then_inc(s_ident, 16)
            sp.dma_start(gin[:, :], norm_g[0].rearrange("(k p) -> p k", p=P), allow_slow_non_contiguous=True).then_inc(s_gin, 16)
            weights(0, 0)
            weights(0, 1)
            sp.dma_start(rot[:, :, :], c_rot).then_inc(s_const, 16)
            sp.dma_start(ctri[:, :], c_bias).then_inc(s_const, 16)
            sp.dma_start(tri[:, :], c_tri).then_inc(s_const, 16)
            sp.dma_start(cols[:, :, :], c_cols).then_inc(s_const, 16)
            sp.dma_start(eye[:, :], c_eye).then_inc(s_const, 16)
            sp.dma_start(iota[:, :], c_iota).then_inc(s_const, 16)
            sp.dma_start(gret[:, :], ret_norm_g[0].rearrange("h e -> e h"), allow_slow_non_contiguous=True).then_inc(s_const, 16)
            for n in range(1, 10):
                weights(n, 0)
                weights(n, 1)
            sp.wait_ge(ki_ev, 4)
            store(nki_p[0, 0].rearrange("(t p) d -> p t d", p=P), kin[:, 0:QT, :])
            store(nki_s[0].rearrange("b o d -> b (o d)"), kin[0:NS, QT, :])
            weights(10, 0)
            weights(10, 1)
            for n in range(11, 13):
                weights(n, 0)
                weights(n, 1)
            sp.wait_ge(kv_ev, 8)
            store(nk_p[0, 0].rearrange("(t p) c d -> p t (c d)", p=P), kan[:, 0:QT, :])
            store(nk_s[0].rearrange("b o c d -> b (o c d)"), kan[0:NS, QT, :])
            store(nv_p[0, 0].rearrange("(t p) c d -> p t (c d)", p=P), van[:, 0:QT, :])
            store(nv_s[0].rearrange("b o c d -> b (o c d)"), van[0:NS, QT, :])
            for n in range(13, 19):
                weights(n, 0)
                weights(n, 1)
            sp.wait_ge(st_out, stores[0])
            for n in (19, 20):
                weights(n, 0)
                weights(n, 1)
            sp.wait_ge(av_mix, NH)
            old_states = lambda h: sp.dma_start(sp_[:, :, :], state_ret[0, :, h].rearrange("b d e -> d b e"))
            old_states(0).then_inc(sp_in, 16)
            for h in range(NH):
                n = 21 + 2 * h
                weights(n, 0)
                weights(n, 1)
                weights(n + 1, 0)
                weights(n + 1, 1)
                sp.wait_ge(s_ready, 4 * h + 4)
                store(st_p[0, 0, h], stt[:, 3, :], st_p_out)
                sp.wait_ge(sn_ready, 2 * h + 2)
                store(st_s[0, :, h].rearrange("b d e -> d b e"), sp_[:, :, :], st_s_out)
                if h < NH - 1:
                    sp.wait_ge(ros_mm, h + 1)
                    sp.wait_ge(st_s_out, 16 * h + 16)
                    old_states(h + 1).then_inc(sp_in, 16)
            sp.wait_ge(st_s_out, 16 * NH)
            sp.wait_ge(st_p_out, 16 * NH)
            sp.wait_ge(sel_f, 1)
            sp.wait_ge(gs_n, 2)
            sp.dma_start(nkb[:, :, :].rearrange("p b c -> p (b c)"),
                         nk_s[0].rearrange("b o c d -> (b o c d)").partition_broadcast(P)
                         ).then_inc(nkb_in, 16)
            sp.wait_ge(kg_fix, 2 * NS)
            sp.dma_start(nkb[:, :, :].rearrange("p b c -> p (b c)"),
                         nv_s[0].rearrange("b o c d -> (b o c d)").partition_broadcast(P)).then_inc(nkb_in, 16)
            sp.wait_ge(mix_ready, 1)
            sp.dma_start(Y[:, :, :], x_prompt[0].rearrange("(t p) m -> p t m", p=P)).then_inc(y_res, 16)
            sp.dma_start(Ys[:, :], x_sample.rearrange("b o m -> (b o) m")).then_inc(y_res, 16)
            sp.dma_start(gfb[:, :], final_norm_g.partition_broadcast(P)).then_inc(y_res, 16)
            for n in range(37, NB):
                weights(n, 0)
                weights(n, 1)
            for i in range(5):
                sp.wait_ge(y_norm, i + 1)
                if i < QT:
                    store(y_prompt[0, P * i:P * i + P, :], Y[:, i, :])
                else:
                    store(y_sample.rearrange("b o m -> (b o) m"), Ys[:, :])
            sp.wait_ge(st_out, stores[0])
            sp.wait_ge(st_p_out, 16 * NH)
            sp.wait_ge(st_s_out, 16 * NH)

        @block.scalar
        def _(act):
            chain = [0]

            def link(ins):
                chain[0] += 1
                ins.then_inc(ach, 1)
                act.wait_ge(ach, chain[0])

            def hi(n, a):
                if n >= NB:
                    return
                act.wait_ge(w_in_sem[a], landed(n))
                if n >= 1:
                    act.wait_ge(a_used, n) if a == 0 else act.wait_ge(acc_done, 4 * n)
                nc.scalar.activation(Wh[:, a, :, 0:width(n)], Wraw[:, a, :, 0:width(n)], ACT.Copy).then_inc(w_hi, 1)

            def evacuate(n):
                for i in range(4):
                    t, half = i // 2, i % 2
                    src = bank[i][:, 0:HALF]
                    s = slice(HALF * half, HALF * half + HALF)
                    act.wait_ge(acc_done, 4 * n + i + 1)
                    if n == 0:
                        ins = nc.scalar.activation((kiT if t == 0 else wiT)[:, s], src, ACT.Copy)
                    elif n <= 8:
                        ins = nc.scalar.activation(mix[:, 2 * (n - 1) + t, s], src, ACT.Copy)
                    elif n <= 10:
                        ins = nc.scalar.activation((kaT if n == 9 else vaT)[:, t, s], src, ACT.Copy)
                    elif n <= 18:
                        j = (n - 11) // 2
                        if n % 2:
                            ins = nc.scalar.activation(mix[:, 2 * j + t, s], src, ACT.Copy)
                        else:
                            ins = nc.scalar.activation(mix[:, NH + 2 * j + t, s], src, ACT.Silu)
                    elif n < NB_IN:
                        h = (n - 19) // 2
                        if n % 2:
                            if i == 0 and h:
                                act.wait_ge(rot_done, 2 * h)
                            nc.scalar.activation(XS[:, t, s], src, ACT.Copy).then_inc(xs_ev, 1)
                            nc.scalar.activation(XW[0:64, t, s], bank[i][64:P, 0:HALF], ACT.Copy).then_inc(xs_ev, 1)
                            ins = nc.scalar.activation(XW[64:P, t, s], bank[i][0:64, 0:HALF], ACT.Copy)
                        elif t == 0:
                            if i == 0 and h:
                                act.wait_ge(vn_tr, 2 * h)
                            ins = nc.scalar.activation(vT[:, s], src, ACT.Copy)
                        else:
                            ins = nc.scalar.activation(mix[:, h, s], src, ACT.Silu)
                    else:
                        if i == 0 and n > NB_IN:
                            act.wait_ge(y_tr, 3 * (n - NB_IN))
                        ins = nc.scalar.activation(yT[:, t, s], src, ACT.Copy)
                    ins.then_inc(acc_free, 1)

            def load_x(i):
                if i >= 2:
                    act.wait_ge(x_tr, 4 * (i - 1))
                if i < QT:
                    act.dma_start(XT[:, i % 2, :], x_prompt[0, P * i:P * i + P, :]).then_inc(x_in[i % 2], 16)
                else:
                    act.dma_start(XT[0:NS, i % 2, :], x_sample.rearrange("b o m -> (b o) m")).then_inc(x_in[i % 2], 16)

            def squares(i):
                act.wait_ge(x_in[i % 2], 16 * (i // 2 + 1))
                r = rows(i)
                if i:
                    act.wait_ge(x_sq, i)
                nc.scalar.activation(junk[0:r, :], XT[0:r, i % 2, :], ACT.Square,
                                     accum_out=st4[0:r, i:i + 1]).then_inc(x_sq, 1)

            load_x(0)
            load_x(1)
            act.dma_start(ptb[:, :, :].rearrange("p b j -> p (b j)"),
                          page_table.rearrange("b j -> (b j)").partition_broadcast(P)).then_inc(s_ptab, 16)
            squares(0)
            for i in range(5):
                if i + 1 < 5:
                    squares(i + 1)
                for g in range(4):
                    v = 4 * i + g
                    act.wait_ge(x_g, v + 1)
                    nc.scalar.activation(Hh[:, 4 * g:4 * g + 4, tok(i)], HT[:, v % 2, :, 0:rows(i)],
                                         ACT.Copy).then_inc(h_hi, 1)
                if i + 2 < 5:
                    load_x(i + 2)
                if i == 0:
                    hi(0, 0)
                    hi(0, 1)
            for n in range(9):
                hi(n + 1, 0)
                evacuate(n)
                hi(n + 1, 1)

            act.wait_ge(ki_tr, 1)
            nc.scalar.activation(kin[:, 0:QT, :].rearrange("p t d -> p (t d)"), bank[4][:, :], ACT.Copy).then_inc(ki_ev, 1)
            act.wait_ge(ki_tr, 2)
            nc.scalar.activation(kin[0:NS, QT, :], bank[5][0:NS, 0:P], ACT.Copy).then_inc(ki_ev, 1)
            act.wait_ge(ki_tr, 3)
            nc.scalar.activation(wn[:, 0:QT, :], bank[6][:, :].rearrange("p (t c) -> p t c", t=QT)[:, :, 112:P],
                                 ACT.Copy, scale=NIH ** -0.5 * SCALE).then_inc(ki_ev, 1)
            act.wait_ge(ki_tr, 4)
            nc.scalar.activation(wn[0:NS, QT, :], bank[7][0:NS, 112:P], ACT.Copy,
                                 scale=NIH ** -0.5 * SCALE).then_inc(ki_ev, 1)
            act.wait_ge(st_out, 32)
            i = 0
            for t in range(1, QT):
                for h in range(NIH):
                    w = P * (t + 1)
                    act.wait_ge(si_mm, i + 1)
                    if i >= 2:
                        act.wait_ge(si_acc, i - 1)
                    nc.scalar.activation(relu[:, i % 2, 0:w], bank[4 + i % 4][:, 0:w], ACT.Relu).then_inc(si_relu, 1)
                    i += 1
            n_si = i
            act.wait_ge(ws_tr, 1)
            nc.scalar.activation(wsel[:, :], bank[0][:, 0:NS], ACT.Copy).then_inc(wsel_ready, 1)
            act.wait_ge(si_acc, n_si)

            def relu_row(c):
                w = T if c < 8 else 1
                act.wait_ge(kt_used, min(NS * (c + 1), 65))
                if c:
                    act.wait_ge(sc_row, c)
                nc.scalar.activation(wiT[:, 0:w], bank[6 + c % 2][:, 0:w], ACT.Relu).then_inc(sc_relu, 1)

            def place_row(c):
                act.wait_ge(sc_row, c + 1)
                if c < 8:
                    nc.scalar.activation(scores[:, T * c:T * c + T].rearrange("b (p q) -> b q p", q=4),
                                         bank[c % 2][0:NS, 0:T].rearrange("b (q p) -> b q p", q=4),
                                         ACT.Copy).then_inc(sc_out, 1)
                else:
                    nc.scalar.activation(scores[:, PAST:NKEY], bank[0][0:NS, 0:1], ACT.Copy).then_inc(sc_out, 1)

            for u in range(64):
                c, b = u // NS, u % NS
                act.wait_ge(kx_tr, u + 1)
                if u >= 2:
                    act.wait_ge(kt_used, u - 1)
                nc.scalar.activation(relu[:, u % 2, :], bank[4 + u % 2][:, :], ACT.Copy).then_inc(kt_ev, 1)
                if c and b == 1:
                    relu_row(c - 1)
                if c and b == 5:
                    place_row(c - 1)
            for c in (7, 8):
                relu_row(c)
                place_row(c)

            for n in (9, 10):
                hi(n + 1, 0)
                if n == 9:
                    act.wait_ge(sc_out, 9)
                evacuate(n)
                hi(n + 1, 1)
            for m in range(4):
                dst = kan if m < 2 else van
                c = slice(P * (m % 2), P * (m % 2) + P)
                act.wait_ge(kv_tr, 2 * m + 1)
                nc.scalar.activation(dst[:, 0:QT, c], bank[4 + m % 2][:, :].rearrange("p (t d) -> p t d", t=QT),
                                     ACT.Copy).then_inc(kv_ev, 1)
                act.wait_ge(kv_tr, 2 * m + 2)
                nc.scalar.activation(dst[0:NS, QT, c], bank[6 + m % 2][0:NS, 0:P], ACT.Copy).then_inc(kv_ev, 1)

            def exps(h):
                for j, t in enumerate((2, 0, 1, 3)):
                    act.wait_ge(al_max, 4 * h + j + 1)
                    r = pb[:, SEG[t]:SEG[t] + P * (t + 1)]
                    nc.scalar.activation(r, r, ACT.Exp, bias=st4[:, 8 + t:9 + t],
                                         accum_out=st4[:, 12 + t:13 + t]).then_inc(al_exp, 1)

            def turned(h):
                if h:
                    act.wait_ge(av_mm, h)
                for j, (a, w) in enumerate(((0, 512), (512, 256), (768, 512))):
                    act.wait_ge(at_tr, 3 * h + j + 1)
                    nc.scalar.activation(pT[:, a:a + w], bank[4 + j][:, 0:w], ACT.Copy).then_inc(at_ev, 1)

            def attention(beta):
                h, what = (beta - 24) // 2, beta % 2
                if beta >= 24:
                    exps(h) if what == 0 else turned(h)

            for n in range(11, 19):
                hi(n + 1, 0)
                attention(2 * n)
                evacuate(n)
                hi(n + 1, 1)
                attention(2 * n + 1)
            exps(7)
            turned(7)

            def normalise(h):
                for c in range(4):
                    act.wait_ge(ro_stat, 4 * h + 4)
                    nc.scalar.activation(nrm[:, c, :], bank[4][:, P * c:P * c + P], ACT.Identity,
                                         bias=st4[:, 24 + c:25 + c], scale=st4[:, 20 + c:21 + c]).then_inc(ro_nrm, 1)
                act.wait_ge(ros_mm, h + 1)
                nc.scalar.activation(OS[:, h, :], bank[5][:, 0:NS], ACT.Copy).then_inc(os_ev, 1)

            act.wait_ge(av_mix, NH)
            act.wait_ge(qb_ready, 1)
            act.wait_ge(st_out, 96)
            for h in range(NH):
                n = 19 + 2 * h
                hi(n + 1, 0)
                if h:
                    normalise(h - 1)
                evacuate(n)
                hi(n + 1, 1)
                hi(n + 2, 0)
                act.wait_ge(kn_tr, 2 * h + 1)
                nc.scalar.activation(kn[:, :, :].rearrange("p c d -> p (c d)"), bank[4][:, :], ACT.Copy,
                                     scale=cols[:, 1, h:h + 1]).then_inc(kn_ev, 1)
                act.wait_ge(kn_tr, 2 * h + 2)
                nc.scalar.activation(kns[:, :], bank[5][0:NS, 0:P], ACT.Copy, scale=SCALE).then_inc(kn_ev, 1)
                evacuate(n + 1)
                act.wait_ge(vn_tr, 2 * h + 1)
                nc.scalar.activation(vn[:, :, :].rearrange("p c d -> p (c d)"), bank[7][:, :], ACT.Copy).then_inc(vn_ev, 1)
                hi(n + 2, 1)
            normalise(NH - 1)

            for b in range(NS):
                act.wait_ge(sk_tr, b + 1)
                if b >= 2:
                    act.wait_ge(sl_mm, b - 1)
                nc.scalar.activation(skT[:, b % 2, :], bank[4 + b % 2][:, :], ACT.Copy).then_inc(sk_ev, 1)
            act.wait_ge(sl_max, 1)
            nc.scalar.activation(sprob[:, :], sprob[:, :], ACT.Exp, bias=st4[0:64, 33:34],
                                 accum_out=st4[0:64, 34:35]).then_inc(sl_exp, 1)
            act.wait_ge(spt_tr, 1)
            nc.scalar.activation(spT[:, :], bank[7][:, 0:P], ACT.Copy).then_inc(spt_ev, 1)

            act.wait_ge(mix_ready, 1)
            for k in range(KT):
                nc.scalar.activation(Hh[:, k, :], mix[:, k, :], ACT.Copy).then_inc(m_hi, 1)
            for n in range(NB_IN, NB):
                hi(n + 1, 0)
                evacuate(n)
                hi(n + 1, 1)
            for i in range(5):
                r = rows(i)
                src = Y[:, i, :] if i < QT else Ys[:, :]
                act.wait_ge(y_add, 3 * 8)
                nc.scalar.activation(mix[0:r, 4:8, 0:T], src, ACT.Square, accum_out=st4[0:r, 40 + i:41 + i]).then_inc(y_sq, 1)
                act.wait_ge(y_sq, i + 1)

        @block.gpsimd
        def _(pool):
            def lo(n, a):
                if n >= NB:
                    return
                pool.wait_ge(w_hi, 2 * n + a + 1)
                w = width(n)
                nc.gpsimd.tensor_tensor(Wl[:, a, :, 0:w], Wraw[:, a, :, 0:w],
                                        Wh[:, a, :, 0:w].bitcast(F32), ALU.subtract).then_inc(w_lo, 1)

            for i in range(5):
                for g in range(4):
                    v = 4 * i + g
                    pool.wait_ge(h_hi, v + 1)
                    nc.gpsimd.tensor_tensor(Hl[:, 4 * g:4 * g + 4, tok(i)], HT[:, v % 2, :, 0:rows(i)],
                                            Hh[:, 4 * g:4 * g + 4, tok(i)].bitcast(F32), ALU.subtract).then_inc(h_lo, 1)
                if i == 0:
                    lo(0, 0)
                    lo(0, 1)
            for n in range(1, 10):
                lo(n, 0)
                lo(n, 1)
            cpages = cache_kidx[0].rearrange("n (r q) d -> (n r) (q d)", q=4)
            pool.wait_ge(pidx_ready, 1)
            for c in range(8):
                for b in range(NS):
                    u = NS * c + b
                    if u >= 4:
                        pool.wait_ge(kx_tr, u - 3)
                    nc.gpsimd.indirect_dma_start(
                        kx[:, u % 4, :], None, cpages,
                        bass.IndirectOffsetOnAxis(ap=pidx[:, b, c:c + 1], axis=0)).then_inc(kx_in[u % 4], 16)
            for n in range(10, 19):
                lo(n, 0)
                lo(n, 1)
            for h in range(NH):
                n = 19 + 2 * h
                lo(n, 0)
                lo(n, 1)
                lo(n + 1, 0)
                for t in range(2):
                    pool.wait_ge(acc_free, 4 * n + 2 * t + 2)
                    nc.gpsimd.tensor_tensor(XS[:, t, :], XS[:, t, :], rot[:, 0, :], ALU.mult).then_inc(pch, 1)
                    nc.gpsimd.tensor_tensor(XW[:, t, :], XW[:, t, :], rot[:, 1, :], ALU.mult).then_inc(pch, 1)
                    pool.wait_ge(pch, 4 * h + 2 * t + 2)
                    if h and t == 0:
                        pool.wait_ge(sT_mm, h)
                    if h and t == 1:
                        pool.wait_ge(ro_mm, h)
                        pool.wait_ge(ros_mm, h)
                    nc.gpsimd.tensor_tensor(kq[:, t, :], XS[:, t, :], XW[:, t, :], ALU.add).then_inc(rot_done, 1)
                lo(n + 1, 1)
            lo(35, 0)
            lo(35, 1)
            kr = cache_k[0].rearrange("n s c d -> (n s) (c d)")
            vr = cache_v[0].rearrange("n s c d -> (n s) (c d)")
            pool.wait_ge(row_ready, 1)
            pool.wait_ge(gs_n, 2)
            pool.wait_ge(st_s_out, 16 * NH)
            pool.wait_ge(st_p_out, 16 * NH)
            for b in range(NS):
                for half in range(2):
                    m = half * NS + b
                    nc.gpsimd.indirect_dma_start(kg[:, m, :], None, kr, bass.IndirectOffsetOnAxis(
                        ap=rowu[:, m:m + 1], axis=0)).then_inc(kg_in[m], 16)
            for b in range(NS):
                for half in range(2):
                    m = half * NS + b
                    nc.gpsimd.indirect_dma_start(vg[:, m, :], None, vr, bass.IndirectOffsetOnAxis(
                        ap=rowu[:, m:m + 1], axis=0)).then_inc(vg_in[m], 16)
            for k in range(KT):
                pool.wait_ge(m_hi, k + 1)
                nc.gpsimd.tensor_tensor(Hl[:, k, :], mix[:, k, :], Hh[:, k, :].bitcast(F32), ALU.subtract).then_inc(m_lo, 1)
            for n in range(36, NB):
                lo(n, 0)
                lo(n, 1)

        @block.vector
        def _(dve):
            chain = [0]

            def link(ins):
                chain[0] += 1
                ins.then_inc(dch, 1)
                dve.wait_ge(dch, chain[0])

            v_ = nc.vector

            def rsqrt(x):
                r, w = x.shape
                y, z = rsq[0:r, 0, 0:w], rsq[0:r, 1, 0:w]
                link(v_.tensor_scalar(y.bitcast(I32), x.bitcast(I32), 1, None, ALU.arith_shift_right))
                link(v_.tensor_scalar(y.bitcast(I32), y.bitcast(I32), -1.0, float(0x5f3759df), ALU.mult, ALU.add))
                for step in range(4):
                    link(v_.tensor_tensor(z, y, y, ALU.mult))
                    link(v_.tensor_tensor(z, z, x, ALU.mult))
                    link(v_.tensor_scalar(z, z, -0.5, 1.5, ALU.mult, ALU.add))
                    link(v_.tensor_tensor(y if step < 3 else x, y, z, ALU.mult))
            for i in range(5):
                r = rows(i)
                dve.wait_ge(x_sq, i + 1)
                link(v_.tensor_scalar(st4[0:r, i:i + 1], st4[0:r, i:i + 1], 1.0 / DM, EPS, ALU.mult, ALU.add))
                rsqrt(st4[0:r, i:i + 1])
                v_.tensor_scalar(XT[0:r, i % 2, :], XT[0:r, i % 2, :], st4[0:r, i:i + 1], None, ALU.mult).then_inc(x_norm, 1)
                if i == 0:
                    dve.wait_ge(s_gin, 16)
                for g in range(4):
                    v = 4 * i + g
                    dve.wait_ge(x_tr, v + 1)
                    if v >= 2:
                        dve.wait_ge(h_lo, v - 1)
                    v_.tensor_tensor(HT[:, v % 2, :, 0:r],
                                     bank[4 + v % 4][:, :].rearrange("p (k t) -> p k t", k=4)[:, :, 0:r],
                                     gin[:, 4 * g:4 * g + 4].unsqueeze(2).to_broadcast([P, 4, r]), ALU.mult).then_inc(x_g, 1)

            dve.wait_ge(s_const, 112)
            dve.wait_ge(s_ptab, 16)
            dve.wait_ge(h_lo, 20)
            for j in range(4):
                src = ptb[32 * j:32 * j + 32, :, :].rearrange("p b (c j) -> p b c j", j=4)[:, :, :, j]
                v_.tensor_copy(pidf[32 * j:32 * j + 32, :, :], src).then_inc(dch, 1)
                chain[0] += 1
            dve.wait_ge(dch, chain[0])
            v_.tensor_scalar(pidx[:, :, :], pidf[:, :, :], 32.0, cols[:, 5, 0:1], ALU.mult, ALU.add).then_inc(pidx_ready, 1)
            link(v_.memset(QS[:, :], 0.0))
            dve.wait_ge(acc_free, 4 * 9)
            v_.tensor_copy(QS[:, :].rearrange("p (b x) -> p b x", x=144)[:, :, 0:NIH],
                           mix[:, :, T:NT].rearrange("p h b -> p b h")).then_inc(qs_ready, 1)
            dve.wait_ge(ki_ev, 4)
            v_.tensor_tensor(wsT[:, :, :], wn[0:NS, QT, :].unsqueeze(1).to_broadcast([NS, NS, NIH]),
                             eye[:, :].unsqueeze(2).to_broadcast([NS, NS, NIH]), ALU.mult).then_inc(ws_ready, 1)
            i = 0
            for t in range(1, QT):
                w = P * (t + 1)
                r = bm[:, SEG[t]:SEG[t] + w]
                for h in range(NIH):
                    dve.wait_ge(si_relu, i + 1)
                    if h:
                        dve.wait_ge(si_acc, i)
                        v_.scalar_tensor_tensor(r, relu[:, i % 2, 0:w], wn[:, t, h:h + 1], r, ALU.mult, ALU.add).then_inc(si_acc, 1)
                    else:
                        v_.tensor_scalar(r, relu[:, i % 2, 0:w], wn[:, t, h:h + 1], None, ALU.mult).then_inc(si_acc, 1)
                    i += 1
            dve.wait_ge(si_acc, i)
            for t in range(1, QT):
                e = bm[:, SEG[t] + P * t:SEG[t] + P * t + P]
                link(v_.tensor_tensor(e, e, ctri[:, :], ALU.add))
            for t in range(1, QT):
                r = bm[:, SEG[t]:SEG[t] + P * (t + 1)]
                for _ in range(SELP // 8):
                    link(v_.max(top8[:, :], r))
                    link(v_.match_replace(r, top8[:, :], r, TAKEN))
                link(v_.tensor_scalar(r, r, TAKEN / 2, NEG, ALU.is_gt, ALU.mult))
            v_.tensor_copy(bm[:, SEG[0]:SEG[0] + P], ctri[:, :]).then_inc(bm_ready, 1)

            rounds = SELS // 8
            done = [0]

            def topk(m):
                for _ in range(m):
                    k = done[0]
                    if k >= 3 * rounds:
                        return
                    row = scores[:, 0:NKEY]
                    if k == 0:
                        dve.wait_ge(sc_out, 9)
                    if k % 3 == 0:
                        link(v_.max(top8[0:NS, :], row))
                    elif k % 3 == 1:
                        link(v_.max_index(idxu[:, 8 * (k // 3):8 * (k // 3) + 8], top8[0:NS, :], row))
                    else:
                        link(v_.match_replace(row, top8[0:NS, :], row, TAKEN))
                    done[0] += 1

            def logits(h):
                for j, (a, w) in enumerate(((0, 512), (512, 256), (768, 512))):
                    dve.wait_ge(al_mm, 3 * h + j + 1)
                    if h:
                        dve.wait_ge(at_tr, 3 * h)
                    v_.scalar_tensor_tensor(pb[:, a:a + w], bank[4 + j][:, 0:w], SCALE, bm[:, a:a + w],
                                            ALU.mult, ALU.add).then_inc(al_bias, 1)
                for j, t in enumerate((2, 0, 1, 3)):
                    dve.wait_ge(al_bias, 3 * h + (1, 1, 2, 3)[j])
                    link(v_.tensor_reduce(st4[:, 8 + t:9 + t], pb[:, SEG[t]:SEG[t] + P * (t + 1)], AXX, ALU.max))
                    v_.tensor_scalar(st4[:, 8 + t:9 + t], st4[:, 8 + t:9 + t], -1.0, None, ALU.mult).then_inc(al_max, 1)
                for j, t in enumerate((2, 0, 1, 3)):
                    dve.wait_ge(al_exp, 4 * h + j + 1)
                    link(v_.reciprocal(st4[:, 16 + t:17 + t], st4[:, 12 + t:13 + t]))
                    r = pb[:, SEG[t]:SEG[t] + P * (t + 1)]
                    v_.tensor_scalar(r, r, st4[:, 16 + t:17 + t], None, ALU.mult).then_inc(p_ready, 1)

            def gate(h):
                dve.wait_ge(av_mm, h + 1)
                dve.wait_ge(acc_free, 4 * (12 + 2 * (h // 2)) + 4)
                v_.tensor_tensor(mix[:, NH + h, 0:T], bank[7][:, :], mix[:, NH + h, 0:T], ALU.mult).then_inc(av_mix, 1)

            topk(6)
            for beta in range(24, 38):
                h = (beta - 24) // 2
                if beta % 2 == 0:
                    if h:
                        gate(h - 1)
                    logits(h)
                topk(2)
            gate(6)
            logits(7)
            gate(7)
            link(v_.memset(QB[:, :], 0.0))
            v_.tensor_copy(QB[:, :].rearrange("p (b c x) -> p b c x", b=NS, c=NKV)[:, :, :, 0:NG],
                           mix[:, 0:NH, T:NT].rearrange("p (c g) b -> p b c g", c=NKV)).then_inc(qb_ready, 1)

            def stats(h):
                dve.wait_ge(ro_mm, h + 1)
                if h:
                    dve.wait_ge(ro_nrm, 4 * h)
                for c in range(4):
                    link(v_.bn_stats(bnst[:, c, :], bank[4][:, P * c:P * c + P]))
                    link(v_.bn_aggr(mv[:, c, :], bnst[:, c, :]))
                q = lambda a: st4[:, a:a + 4]
                link(v_.tensor_scalar(q(28), mv[:, :, 1], cols[:, 3, h:h + 1], EPS, ALU.mult, ALU.add))
                rsqrt(q(28))
                link(v_.tensor_scalar(q(20), q(28), cols[:, 2, h:h + 1], None, ALU.mult))
                v_.scalar_tensor_tensor(q(24), mv[:, :, 0], -1.0, q(20), ALU.mult, ALU.mult).then_inc(ro_stat, 4)

            def gated(h):
                dve.wait_ge(rn_tr, h + 1)
                v_.scalar_tensor_tensor(mix[:, h, 0:T], bank[6][:, :], gret[:, h:h + 1], mix[:, h, 0:T],
                                        ALU.mult, ALU.mult).then_inc(rn_mix, 1)

            for h in range(NH):
                if h:
                    stats(h - 1)
                    topk(1)
                    gated(h - 1)
                    topk(3)
                else:
                    topk(4)
                dve.wait_ge(sT_mm, h + 1)
                v_.scalar_tensor_tensor(am[:, :, :], bank[6][:, :].rearrange("p (c i) -> p c i", c=4), cols[:, 0, h:h + 1],
                                        tri[:, :].unsqueeze(1).to_broadcast([P, 4, P]), ALU.mult, ALU.mult).then_inc(am_ready, 1)
                dve.wait_ge(vn_tr, 2 * h + 2)
                v_.tensor_tensor(vx[:, :, :], bank[5][0:NS, 0:P].unsqueeze(1).to_broadcast([NS, NS, P]),
                                 eye[:, :].unsqueeze(2).to_broadcast([NS, NS, P]), ALU.mult).then_inc(vx_ready, 1)
                dve.wait_ge(u_mm, h + 1)
                if h:
                    dve.wait_ge(st_p_out, 16 * h)
                v_.tensor_copy(stt[:, 0, :], bank[4][:, 0:P]).then_inc(s_ready, 1)
                for c in range(1, 4):
                    dve.wait_ge(s_ready, 4 * h + c)
                    v_.scalar_tensor_tensor(stt[:, c, :], stt[:, c - 1, :], cols[:, 4, h:h + 1],
                                            bank[4][:, P * c:P * c + P], ALU.mult, ALU.add).then_inc(s_ready, 1)
                dve.wait_ge(sp_in, 16 * (h + 1))
                for j in range(2):
                    dve.wait_ge(us_mm, 2 * h + j + 1)
                    r = sp_[:, 4 * j:4 * j + 4, :].rearrange("p b e -> p (b e)")
                    v_.scalar_tensor_tensor(r, r, float(1.0 - 2.0 ** (-5 - h)), bank[(5, 7)[j]][:, :],
                                            ALU.mult, ALU.add).then_inc(sn_ready, 1)
                topk(4)
            stats(NH - 1)
            gated(NH - 1)
            dve.wait_ge(gs_tr, 1)
            link(v_.bn_stats(bnst[0:64, 0, :], bank[7][0:64, 0:P]))
            link(v_.bn_aggr(mv[0:64, 0, :], bnst[0:64, 0, :]))
            link(v_.tensor_scalar(st4[0:64, 28:29], mv[0:64, 0, 1:2], EPS, None, ALU.add))
            rsqrt(st4[0:64, 28:29])
            v_.tensor_scalar(nrm[0:64, 0, :], bank[7][0:64, 0:P], mv[0:64, 0, 0:1], st4[0:64, 28:29],
                             ALU.subtract, ALU.mult).then_inc(gs_n, 1)
            dve.wait_ge(gs_tr, 2)
            link(v_.tensor_tensor(nrm[:, 1, 0:64].rearrange("p (h b) -> p h b", h=NH),
                                  bank[7][:, 0:64].rearrange("p (h b) -> p h b", h=NH),
                                  gret[:, :].unsqueeze(2).to_broadcast([P, NH, NS]), ALU.mult))
            v_.tensor_tensor(mix[:, 0:NH, T:NT], nrm[:, 1, 0:64].rearrange("p (h b) -> p h b", h=NH),
                             mix[:, 0:NH, T:NT], ALU.mult).then_inc(gs_n, 1)
            topk(3 * rounds)

            dve.wait_ge(gs_n, 2)
            dve.wait_ge(st_s_out, 16 * NH)
            dve.wait_ge(st_p_out, 16 * NH)
            v_.tensor_copy(sidf[:, :], idxu[:, :]).then_inc(sel_f, 1)
            dve.wait_ge(sel_tr, 1)
            pos = posf[:, :, :].rearrange("p a b -> p (a b)")
            link(v_.tensor_copy(pos, bank[6][:, 0:2 * NS]))
            ia = [posi[:, k, :] for k in range(4)]
            link(v_.tensor_scalar(ia[3], pos, float(PAST) - 0.5, None, ALU.is_gt))
            link(v_.tensor_scalar(ia[0], pos, float(PAST - 1), None, ALU.min))
            link(v_.tensor_scalar(ia[1], ia[0], 7, None, ALU.arith_shift_right))
            link(v_.tensor_scalar(ia[2], ia[0], P - 1, None, ALU.bitwise_and))
            link(v_.tensor_copy(posw[:, 0, :], ia[1]))
            link(v_.tensor_tensor(ohot[:, :, :], iota[:, :].unsqueeze(1).to_broadcast([P, 2 * NS, PAGES]),
                                  posw[:, 0, :].unsqueeze(2).to_broadcast([P, 2 * NS, PAGES]), ALU.is_equal))
            for half in range(2):
                o_ = ohot[:, NS * half:NS * half + NS, :]
                link(v_.tensor_tensor(o_, o_, ptb[:, :, :], ALU.mult))
            link(v_.tensor_reduce(posw[:, 0, :], ohot[:, :, :], AXX, ALU.add))
            link(v_.tensor_copy(posw[:, 1, :], ia[2]))
            v_.scalar_tensor_tensor(rowu[:, :], posw[:, 0, :], float(P), posw[:, 1, :], ALU.mult, ALU.add).then_inc(row_ready, 1)
            for what, buf, s, fix in ((0, kg, kg_in, kg_fix), (1, vg, vg_in, vg_fix)):
                dve.wait_ge(nkb_in, 16 * (what + 1))
                for b in range(NS):
                    for half in range(2):
                        m = half * NS + b
                        dve.wait_ge(s[m], 16)
                        v_.copy_predicated(buf[:, m, :], ia[3][:, m:m + 1].to_broadcast([P, 256]), nkb[:, b, :]).then_inc(fix, 1)
                if what == 0:
                    dve.wait_ge(sl_mm, NS)
                    link(v_.tensor_scalar(sprob[:, :], bank[6][0:64, 0:SELS], SCALE, None, ALU.mult))
                    link(v_.tensor_reduce(st4[0:64, 33:34], sprob[:, :], AXX, ALU.max))
                    v_.tensor_scalar(st4[0:64, 33:34], st4[0:64, 33:34], -1.0, None, ALU.mult).then_inc(sl_max, 1)
                    dve.wait_ge(sl_exp, 1)
                    link(v_.reciprocal(st4[0:64, 35:36], st4[0:64, 34:35]))
                    v_.tensor_scalar(sprob[:, :], sprob[:, :], st4[0:64, 35:36], None, ALU.mult).then_inc(sp_ready, 1)
            dve.wait_ge(so_mm, 1)
            v_.tensor_tensor(mix[:, NH:KT, T:NT], bank[4][:, 0:64].rearrange("p (b h) -> p h b", b=NS),
                             mix[:, NH:KT, T:NT], ALU.mult).then_inc(mix_ready, 1)

            dve.wait_ge(y_res, 48)
            for k in range(8):
                c = slice(256 * k, 256 * k + 256)
                for j in range(2):
                    dve.wait_ge(y_tr, 3 * k + j + 1)
                    r = Y[:, 2 * j:2 * j + 2, c]
                    v_.tensor_tensor(r, r, bank[4 + j][:, :].rearrange("p (t m) -> p t m", t=2), ALU.add).then_inc(y_add, 1)
                dve.wait_ge(y_tr, 3 * k + 3)
                v_.tensor_tensor(Ys[:, c], Ys[:, c], bank[6][0:NS, 0:256], ALU.add).then_inc(y_add, 1)
            for i in range(5):
                r = rows(i)
                y = Y[:, i, :] if i < QT else Ys[:, :]
                s = st4[0:r, 40 + i:41 + i]
                dve.wait_ge(y_sq, i + 1)
                link(v_.tensor_scalar(s, s, 1.0 / DM, EPS, ALU.mult, ALU.add))
                rsqrt(s)
                v_.scalar_tensor_tensor(y, y, s, gfb[0:r, :], ALU.mult, ALU.mult).then_inc(y_norm, 1)

        @block.tensor
        def _(pe):
            mm = nc.tensor.matmul

            def chunk(n, a):
                pe.wait_ge(w_lo, 2 * n + a + 1)
                for i in range(4):
                    t, half = i // 2, i % 2
                    s = slice(HALF * half, HALF * half + HALF)
                    if a == 0 and n >= 1:
                        pe.wait_ge(acc_free, 4 * (n - 1) + i + 1)
                    for k in range(KC):
                        kk = KC * a + k
                        if n == NB_IN and i == 0:
                            pe.wait_ge(m_lo, kk + 1)
                        wh, wl = Wh[:, a, k, tile_cols(n, t)], Wl[:, a, k, tile_cols(n, t)]
                        mm(bank[i][:, 0:HALF], wh, Hh[:, kk, s], start=(kk == 0), stop=False)
                        mm(bank[i][:, 0:HALF], wh, Hl[:, kk, s], start=False, stop=False)
                        last = mm(bank[i][:, 0:HALF], wl, Hh[:, kk, s], start=False, stop=(kk == KT - 1))
                    if a == 1:
                        last.then_inc(acc_done, 1)
                if a == 0:
                    last.then_inc(a_used, 1)

            def turn(out, in_, k=P):
                return nc.tensor.transpose(out, in_, ident[0:k, 0:k])

            pe.wait_ge(s_ident, 16)
            for i in range(5):
                r = rows(i)
                pe.wait_ge(x_norm, i + 1)
                for g in range(4):
                    v = 4 * i + g
                    if v >= 4:
                        pe.wait_ge(x_g, v - 3)
                    for k in range(4):
                        c = P * (4 * g + k)
                        last = turn(bank[4 + v % 4][:, P * k:P * k + r], XT[0:r, i % 2, c:c + P], r)
                    last.then_inc(x_tr, 1)
            pe.wait_ge(h_lo, 20)
            for n in range(9):
                chunk(n, 0)
                chunk(n, 1)

            for q, src in ((0, kiT), (2, wiT)):
                for t in range(QT):
                    last = turn(bank[4 + q][:, P * t:P * t + P], src[:, tok(t)])
                last.then_inc(ki_tr, 1)
                turn(bank[5 + q][0:NS, 0:P], src[:, T:NT]).then_inc(ki_tr, 1)
            pe.wait_ge(ki_ev, 4)
            pe.wait_ge(acc_free, 36)
            i = 0
            for t in range(1, QT):
                for h in range(NIH):
                    w = P * (t + 1)
                    if i >= 4:
                        pe.wait_ge(si_relu, i - 3)
                    mm(bank[4 + i % 4][:, 0:w], mix[:, h, tok(t)], kiT[:, 0:w], start=True, stop=True).then_inc(si_mm, 1)
                    i += 1
            pe.wait_ge(ws_ready, 1)
            turn(bank[0][:, 0:NS], wsT[:, :, :].rearrange("a b h -> a (b h)"), NS).then_inc(ws_tr, 1)
            pe.wait_ge(si_relu, i)
            pe.wait_ge(qs_ready, 1)
            qs = QS[:, 0:NS * P].rearrange("p (b m) -> p b m", b=NS)

            def turn_keys(u):
                pe.wait_ge(kx_in[u % 4], 16 * (u // 4 + 1))
                if u >= 2:
                    pe.wait_ge(kt_ev, u - 1)
                for q in range(4):
                    last = turn(bank[4 + u % 2][:, P * q:P * q + P], kx[:, u % 4, P * q:P * q + P])
                last.then_inc(kx_tr, 1)

            def row_product(c):
                w = T if c < 8 else 1
                pe.wait_ge(sc_relu, c + 1)
                pe.wait_ge(wsel_ready, 1)
                if c >= 2:
                    pe.wait_ge(sc_out, c - 1)
                mm(bank[c % 2][0:NS, 0:w], wsel[:, :], wiT[:, 0:w], start=True, stop=True).then_inc(sc_row, 1)

            turn_keys(0)
            for u in range(64):
                c, b = u // NS, u % NS
                if u + 1 < 64:
                    turn_keys(u + 1)
                pe.wait_ge(kt_ev, u + 1)
                if b == 0 and c >= 2:
                    pe.wait_ge(sc_relu, c - 1)
                last = mm(bank[6 + c % 2][:, :], qs[:, b, :], relu[:, u % 2, :], start=(b == 0), stop=(b == NS - 1))
                last.then_inc(kt_used, 1)
                if b == 3 and c >= 1:
                    row_product(c - 1)
            pe.wait_ge(sc_relu, 7)
            for b in range(NS):
                last = mm(bank[6][:, 0:1], qs[:, b, :], kiT[:, T + b:T + b + 1], start=(b == 0), stop=(b == NS - 1))
            last.then_inc(kt_used, 1)
            row_product(7)
            row_product(8)
            pe.wait_ge(sc_out, 9)

            for n in (9, 10):
                chunk(n, 0)
                chunk(n, 1)
            pe.wait_ge(acc_free, 44)
            for m in range(4):
                src = (kaT if m < 2 else vaT)[:, m % 2, :]
                if m >= 2:
                    pe.wait_ge(kv_ev, 2 * m - 2)
                for t in range(QT):
                    last = turn(bank[4 + m % 2][:, P * t:P * t + P], src[:, tok(t)])
                last.then_inc(kv_tr, 1)
                turn(bank[6 + m % 2][0:NS, 0:P], src[:, T:NT]).then_inc(kv_tr, 1)

            def query_key(h):
                pe.wait_ge(bm_ready, 1)
                pe.wait_ge(acc_free, 4 * (11 + 2 * (h // 2)) + 4)
                if h == 0:
                    pe.wait_ge(kv_ev, 8)
                else:
                    pe.wait_ge(at_ev, 3 * h)
                for t, bk, o_ in ((2, 4, 0), (0, 4, 384), (1, 5, 0), (3, 6, 0)):
                    w = P * (t + 1)
                    last = mm(bank[bk][:, o_:o_ + w], mix[:, h, tok(t)], kaT[:, h // NG, 0:w], start=True, stop=True)
                    if t != 2:
                        last.then_inc(al_mm, 1)

            def turn_probs(h):
                pe.wait_ge(p_ready, 4 * h + 4)
                for bk, a, w in ((4, 0, 512), (5, 512, 256), (6, 768, 512)):
                    for k in range(w // P):
                        last = turn(bank[bk][:, P * k:P * k + P], pb[:, a + P * k:a + P * k + P])
                    last.then_inc(at_tr, 1)

            def prob_value(h):
                pe.wait_ge(at_ev, 3 * h + 3)
                if h:
                    pe.wait_ge(av_mix, h)
                c = P * (h // NG)
                for t in range(QT):
                    for s in range(t + 1):
                        last = mm(bank[7][:, P * t:P * t + P], van[:, s, c:c + P],
                                  pT[:, SEG[t] + P * s:SEG[t] + P * s + P], start=(s == 0), stop=(s == t))
                last.then_inc(av_mm, 1)

            for n in range(11, 19):
                for a in range(2):
                    chunk(n, a)
                    beta = 2 * n + a
                    if beta >= 24:
                        h = (beta - 24) // 2
                        if beta % 2 == 0:
                            if h:
                                prob_value(h - 1)
                            query_key(h)
                        else:
                            turn_probs(h)
            prob_value(6)
            query_key(7)
            turn_probs(7)
            prob_value(7)

            def outputs(h):
                pe.wait_ge(am_ready, h + 1)
                pe.wait_ge(s_ready, 4 * h + 4)
                for c in range(4):
                    o_ = bank[4][:, P * c:P * c + P]
                    last = mm(o_, am[:, c, :], vn[:, c, :], start=True, stop=(c == 0))
                    if c:
                        last = mm(o_, kq[:, 1, tok(c)], stt[:, c - 1, :], start=False, stop=True)
                last.then_inc(ro_mm, 1)
                pe.wait_ge(sn_ready, 2 * h + 2)
                for b in range(NS):
                    last = mm(bank[5][:, b:b + 1], sp_[:, b, :], kq[:, 1, T + b:T + b + 1], start=True, stop=True)
                last.then_inc(ros_mm, 1)

            def turn_outputs(h):
                pe.wait_ge(ro_nrm, 4 * h + 4)
                pe.wait_ge(am_ready, h + 1)
                for c in range(4):
                    last = turn(bank[6][:, P * c:P * c + P], nrm[:, c, :])
                last.then_inc(rn_tr, 1)

            for h in range(NH):
                n = 19 + 2 * h
                chunk(n, 0)
                if h:
                    outputs(h - 1)
                chunk(n, 1)
                if h:
                    turn_outputs(h - 1)
                chunk(n + 1, 0)
                pe.wait_ge(rot_done, 2 * h + 1)
                if h:
                    pe.wait_ge(os_ev, h)
                for c in range(4):
                    last = turn(bank[4][:, P * c:P * c + P], kq[:, 0, tok(c)])
                last.then_inc(kn_tr, 1)
                turn(bank[5][0:NS, 0:P], kq[:, 0, T:NT]).then_inc(kn_tr, 1)
                chunk(n + 1, 1)
                pe.wait_ge(rot_done, 2 * h + 2)
                if h:
                    pe.wait_ge(rn_mix, h)
                for c in range(4):
                    last = mm(bank[6][:, P * c:P * c + P], kq[:, 0, tok(c)], kq[:, 1, tok(c)], start=True, stop=True)
                last.then_inc(sT_mm, 1)
                pe.wait_ge(acc_free, 4 * (n + 1) + 2)
                pe.wait_ge(kn_ev, 2 * h + 2)
                pe.wait_ge(sn_ready, 2 * h) if h else pe.wait_ge(av_mix, NH)
                for c in range(4):
                    last = turn(bank[7][:, P * c:P * c + P], vT[:, tok(c)])
                last.then_inc(vn_tr, 1)
                turn(bank[5][0:NS, 0:P], vT[:, T:NT]).then_inc(vn_tr, 1)
                pe.wait_ge(vn_ev, h + 1)
                for c in range(4):
                    last = mm(bank[4][:, P * c:P * c + P], kn[:, c, :], vn[:, c, :], start=True, stop=True)
                last.then_inc(u_mm, 1)
                pe.wait_ge(vx_ready, h + 1)
                for j in range(2):
                    mm(bank[(5, 7)[j]][:, :], kns[:, :], vx[:, 4 * j:4 * j + 4, :].rearrange("p b e -> p (b e)"),
                       start=True, stop=True).then_inc(us_mm, 1)
            outputs(NH - 1)
            turn_outputs(NH - 1)
            pe.wait_ge(os_ev, NH)
            pe.wait_ge(sn_ready, 2 * NH)
            turn(bank[7][0:64, 0:P], OS[:, :, :].rearrange("p h b -> p (h b)")).then_inc(gs_tr, 1)
            pe.wait_ge(gs_n, 1)
            turn(bank[7][:, 0:64], nrm[0:64, 0, :], 64).then_inc(gs_tr, 1)

            pe.wait_ge(sel_f, 1)
            pe.wait_ge(rn_mix, NH)
            for half in range(2):
                last = turn(bank[6][:, NS * half:NS * half + NS], sidf[:, P * half:P * half + P], NS)
            last.then_inc(sel_tr, 1)
            pe.wait_ge(qb_ready, 1)
            qb = QB[:, 0:1024].rearrange("p (m x) -> p m x", x=64)
            pe.wait_ge(row_ready, 1)
            pe.wait_ge(os_ev, NH)

            def turn_selected(b):
                pe.wait_ge(kg_fix, 2 * b + 2)
                if b >= 2:
                    pe.wait_ge(sk_ev, b - 1)
                for c in range(NKV):
                    for half in range(2):
                        k = 2 * c + half
                        last = turn(bank[4 + b % 2][:, P * k:P * k + P], kg[:, half * NS + b, P * c:P * c + P])
                last.then_inc(sk_tr, 1)

            turn_selected(0)
            for b in range(NS):
                if b + 1 < NS:
                    turn_selected(b + 1)
                pe.wait_ge(sk_ev, b + 1)
                for c in range(NKV):
                    last = mm(bank[6][0:64, 0:SELS], qb[:, 2 * b + c, :], skT[:, b % 2, SELS * c:SELS * c + SELS],
                              start=(b == 0 and c == 0), stop=(b == NS - 1 and c == 1))
                last.then_inc(sl_mm, 1)
            pe.wait_ge(sp_ready, 1)
            for half in range(2):
                last = turn(bank[7][:, 64 * half:64 * half + 64], sprob[:, P * half:P * half + P], 64)
            last.then_inc(spt_tr, 1)
            pe.wait_ge(spt_ev, 1)
            for b in range(NS):
                pe.wait_ge(vg_fix, 2 * b + 2)
                for c in range(NKV):
                    o_ = NH * b + NG * c
                    for half in range(2):
                        last = mm(bank[4][:, o_:o_ + NG], vg[:, half * NS + b, P * c:P * c + P],
                                  spT[:, 64 * half + o_:64 * half + o_ + NG], start=(half == 0), stop=(half == 1))
            last.then_inc(so_mm, 1)

            def turn_y(k):
                pe.wait_ge(acc_free, 4 * (NB_IN + k) + 4)
                if k:
                    pe.wait_ge(y_add, 3 * k)
                for j in range(2):
                    for t in range(2):
                        for m in range(2):
                            last = turn(bank[4 + j][:, 256 * t + P * m:256 * t + P * m + P], yT[:, m, tok(2 * j + t)])
                    last.then_inc(y_tr, 1)
                for m in range(2):
                    last = turn(bank[6][0:NS, P * m:P * m + P], yT[:, m, T:NT])
                last.then_inc(y_tr, 1)

            for n in range(NB_IN, NB):
                chunk(n, 0)
                if n > NB_IN:
                    turn_y(n - NB_IN - 1)
                chunk(n, 1)
            turn_y(7)


_CONSTS = None


def _tables():
    import numpy as np
    half = 64
    inv = np.float32(10000.0) ** (-np.arange(half, dtype=np.float32) / np.float32(half))
    pos = np.concatenate([np.arange(512), np.full(8, 4096)]).astype(np.float32)
    ang = (inv[:, None].astype(np.float32) * pos[None, :]).astype(np.float32).astype(np.float64)
    rot = np.zeros((128, 2, 520), np.float32)
    rot[0:64, 0] = rot[64:128, 0] = np.cos(ang)
    rot[0:64, 1] = -np.sin(ang)
    rot[64:128, 1] = np.sin(ang)
    j = np.arange(128, dtype=np.float64)
    tri = (j[None, :] >= j[:, None]).astype(np.float32)
    bias = np.where(j[None, :] <= j[:, None], 0.0, -1e30).astype(np.float32)
    cols = np.zeros((128, 6, 8), np.float32)
    for h in range(8):
        lg = np.log1p(-2.0 ** (-5.0 - h))
        cols[:, 0, h] = 128.0 ** -0.5 * np.exp(-(j + 1) * lg)
        cols[:, 1, h] = 128.0 ** -0.5 * np.exp((127 - j) * lg)
        cols[:, 2, h] = np.exp((j + 1) * lg)
        cols[:, 3, h] = np.exp(2 * (j + 1) * lg)
        cols[:, 4, h] = np.exp(128 * lg)
        cols[:, 5, h] = j % 32
    return {"c_ident": np.eye(128, dtype=np.float32), "c_rot": rot, "c_tri": tri, "c_bias": bias, "c_cols": cols,
            "c_eye": np.eye(8, dtype=np.float32),
            "c_iota": np.tile(np.arange(32, dtype=np.float32), (128, 1))}


_INS = ["x_prompt", "x_sample", "cache_k", "cache_v", "cache_kidx", "state_ret", "page_table", "norm_g", "w_in",
        "ret_norm_g", "w_out", "final_norm_g"]
_OUTS = [(1, 512, 2048), (8, 1, 2048), (1, 1, 512, 2, 128), (1, 1, 512, 2, 128), (1, 1, 512, 128),
         (1, 1, 8, 128, 128), (1, 8, 1, 2, 128), (1, 8, 1, 2, 128), (1, 8, 1, 128), (1, 8, 8, 128, 128)]


def kernel(**inputs):
    import numpy as np
    import concourse.bacc as bacc
    from concourse.bass_utils import run_bass_kernel_spmd

    nc = bacc.Bacc("TRN2", target_bir_lowering=False, num_devices=1)
    arrays, args = {}, []
    given = {name: np.ascontiguousarray(inputs[name]) for name in _INS}
    given.update(_tables())
    for name, a in given.items():
        arrays[f"in_{name}"] = a
        args.append(nc.dram_tensor(f"in_{name}", a.shape, mybir.dt.from_np(a.dtype), kind="ExternalInput").ap())
    for i, shape in enumerate(_OUTS):
        args.append(nc.dram_tensor(f"out_{i}", shape, F32, kind="ExternalOutput").ap())
    build(nc, *args)
    r = run_bass_kernel_spmd(nc, [arrays], core_ids=[0])
    return tuple(r.results[0][f"out_{i}"] for i in range(len(_OUTS)))
```

```python
import concourse.bass as bass
from concourse import mybir
from concourse.alu_op_type import AluOpType as ALU
from contextlib import ExitStack

F32 = mybir.dt.float32
F32R = mybir.dt.float32r
I32 = mybir.dt.int32
U32 = mybir.dt.uint32
ACT = mybir.ActivationFunctionType
AXX = mybir.AxisListType.X

P = 128
DM = 2048
T = 512
NS = 8
NT = T + NS
HALF = NT // 2
KT = DM // P
KC = KT // 2
NH = 8
NKV = 2
NG = NH // NKV
NIH = 16
PAGES = 32
PAST = PAGES * P
NKEY = PAST + 1
SELP = 128
SELS = 256
EPS = 1e-6
NEG = -1e30
TAKEN = -3e38
SCALE = P ** -0.5
NB_IN, NB = 35, 43
QT = T // P
SEG = {2: 0, 0: 384, 1: 512, 3: 768}
SEGW = 1280
LASTC = DM - 256
SEC = 4
SKEY = PAST // SEC
SPG = PAGES // SEC
KPR = SKEY // P
RPP = P // KPR
HP = 2
NEWROW = float(1 << 22)


def build(nc, x_prompt, x_sample, cache_k, cache_v, cache_kidx, state_ret, page_table, norm_g, w_in,
          ret_norm_g, w_out, final_norm_g, c_ident, c_rot, c_tri, c_bias, c_cols, c_eye,
          y_prompt, y_sample, nk_p, nv_p, nki_p, st_p, nk_s, nv_s, nki_s, st_s):
    ctx = ExitStack()
    with ctx:
        def sb(name, shape, dt=F32):
            return ctx.enter_context(nc.sbuf_tensor(name, shape, dt))

        def sem(name):
            return ctx.enter_context(nc.semaphore(name))

        Hh = sb("Hh", [P, KT, NT], F32R)
        Hl = sb("Hl", [P, KT, NT], F32R)
        Wraw = sb("Wraw", [P, 2, KC, 256])
        Wh = sb("Wh", [P, 2, KC, 256], F32R)
        Wl = sb("Wl", [P, 2, KC, 256], F32R)
        mix = sb("mix", [P, KT, NT])
        ident = sb("ident", [P, P])
        rot = sb("rot", [P, 2, NT])
        tri = sb("tri", [P, P])
        cols = sb("cols", [P, 8, NH])
        ctri = sb("ctri", [P, P])
        eye = sb("eye", [NS, NS])
        gains_T = sb("gains_T", [P, KT + NH])
        gin = gains_T[:, 0:KT]
        gret = gains_T[:, KT:KT + NH]
        ptb = sb("ptb", [P, NS, PAGES], I32)
        pti = sb("pti", [NS * SEC, SPG], I32)
        ptf = sb("ptf", [NS * SEC, SPG + 1])
        QB = sb("QB", [P, 16 * 20])
        posu = sb("posu", [P, 2 * NS], U32)
        rowf = sb("rowf", [P, 2 * NS])
        rowu = sb("rowu", [P, 2 * NS], U32)
        isnew = sb("isnew", [P, 2 * NS], I32)
        st4 = sb("st4", [P, 64])
        rsq = sb("rsq", [P, 2, 8])
        ysq = sb("ysq", [P, 5, 8])
        bnst = sb("bnst", [P, 4, 6])
        mv = sb("mv", [P, 4, 2])
        top8 = sb("top8", [P, 8])
        OS = sb("OS", [P, NH, NS])

        base = nc.sbuf_base
        base = (base + 31) // 32 * 32
        room = nc.sbuf_usable_end - 32 - base
        at = {}

        def place(name, shape, dt, off):
            n = 4
            for s in shape[1:]:
                n *= s
            off = (off + 31) // 32 * 32
            assert off + n <= room, (name, off, n, room)
            at[name] = (off, n)
            return nc.alloc_sbuf_tensor_at(name, shape, dt, offset=base + off), off + n

        XT, o = place("XT", [P, 5, DM], F32, 0)
        HT, o = place("HT", [P, 4, 4, P], F32, o)
        gn, o = place("gn", [KT + NH, P], F32, o)
        scores, o = place("scores", [NS * SEC, SKEY + 4], F32, 0)
        cand, _ = place("cand", [NS, SEC * SELS], F32, 0)
        best, o = place("best", [NS * SEC, SELS], F32, o)
        besti, o = place("besti", [NS * SEC, SELS], U32, o)
        brow, o = place("brow", [NS * SEC, SELS], F32, o)
        bpage, o = place("bpage", [NS * SEC, SELS], F32, o)
        bterm, o = place("bterm", [NS * SEC, SELS], F32, o)
        persist = o
        bm, o = place("bm", [P, SEGW], F32, persist)
        after_bm = o
        kiT, o = place("kiT", [P, NT], F32, o)
        wiT, o = place("wiT", [P, NT], F32, o)
        wn, o = place("wn", [P, 5, NIH], F32, o)
        kin, _ = place("kin", [P, 5, P], F32, o)
        relu, o2 = place("relu", [P, 2, T], F32, o)
        kT, o3 = place("kT", [P, 6, T], F32, o)
        QS, o3 = place("QS", [P, NS * 32], F32, o3)
        wsT, o3 = place("wsT", [NS, 2, 4, 32], F32, o3)
        wsel, o3 = place("wsel", [P, 2, SEC * (NS * SEC + NS)], F32, o3)
        pidx, o3 = place("pidx", [P, NS, SEC], U32, o3)
        pidf, o3 = place("pidf", [P, NS, SEC], F32, o3)
        relu2, o3 = place("relu2", [P, T], F32, o3)
        ptm, _ = place("ptm", [P, NS * SEC, SPG], F32, at["relu2"][0])
        kx = []
        for i in range(6):
            off = (at["scores"][0], at["best"][0])[i] if i < 2 else o3
            t_, o4 = place(f"kx{i}", [P, KPR * P], F32, off)
            kx.append(t_)
            o3 = o4 if i >= 2 else o3
        assert at["kx1"][0] + 4 * KPR * P <= persist
        kaT, o = place("kaT", [P, NKV, NT], F32, after_bm)
        after_kaT = o
        kg, o = place("kg", [P, 4, 256], F32, 0)
        vg, o = place("vg", [P, 4, 256], F32, o)
        nkb, o = place("nkb", [P, 2, 2, 256], F32, o)
        skT, o = place("skT", [P, 2, 512], F32, o)
        sprob, o = place("sprob", [16, SELS], F32, o)
        spT, o = place("spT", [P, 2, 16], F32, o)
        o = max(o, after_kaT)
        XS, _ = place("XS", [P, 2, NT], F32, o)
        vx, _ = place("vx", [NS, NS, P], F32, o)
        XW, o = place("XW", [P, 2, NT], F32, o + 8 * NT)
        kq, o = place("kq", [P, 2, NT], F32, o)
        vT, o = place("vT", [P, NT], F32, o)
        kn, o = place("kn", [P, 4, P], F32, o)
        vn, o = place("vn", [P, 4, P], F32, o)
        am, o = place("am", [P, 4, P], F32, o)
        nrm, o = place("nrm", [P, 4, P], F32, o)
        stt, o = place("stt", [P, 4, P], F32, o)
        sp_, o = place("sp_", [P, NS, P], F32, o)
        kns, o = place("kns", [NS, P], F32, o)
        sidf, _ = place("sidf", [NS, SELS], F32, o)
        van, o = place("van", [P, 5, NKV * P], F32, at["vT"][0])
        pb, o = place("pb", [P, SEGW], F32, o)
        pT, o = place("pT", [P, SEGW], F32, o)
        vaT, o = place("vaT", [P, NKV, NT], F32, after_kaT)
        kan, o = place("kan", [P, 5, NKV * P], F32, o)
        assert o <= at["van"][0] and after_kaT <= at["XS"][0]
        Y, o = place("Y", [P, QT, DM], F32, 0)
        Ys, o = place("Ys", [NS, DM], F32, o)
        gfb, o = place("gfb", [P, DM], F32, o)
        row_table = nc.dram_tensor("row_table", (NS * SEC * SELS, 1), F32).ap()
        tabv = row_table.rearrange("(b s r) o -> s b (r o)", b=NS, s=SEC)
        yT = mix[:, 0:2, :]

        bank = [ctx.enter_context(nc.psum_tensor(f"bank{i}", [P, 512], F32)) for i in range(8)]

        s_const = sem("s_const"); s_ident = sem("s_ident"); s_gin = sem("s_gin"); s_ptab = sem("s_ptab")
        x_in = [sem(f"x_in{i}") for i in range(5)]
        x_sq = sem("x_sq"); st4_set = sem("st4_set"); g_tr = sem("g_tr"); x_norm = sem("x_norm"); x_tr = sem("x_tr"); x_g = sem("x_g")
        h_hi = sem("h_hi"); h_lo = sem("h_lo")
        w_in_sem = [sem("w_landed0"), sem("w_landed1")]
        w_hi = sem("w_hi"); w_lo = sem("w_lo"); a_used = sem("chunk_a_used")
        acc_done = sem("acc_done"); acc_free = sem("acc_free")
        dch = sem("dve_chain"); ach = sem("act_chain"); pch = sem("pool_chain")
        st_out = sem("stores_done")
        ki_tr = sem("ki_tr"); ki_ev = sem("ki_ev")
        si_mm = sem("si_mm"); si_relu = sem("si_relu"); si_acc = sem("si_acc")
        ws_ready = sem("ws_ready"); ws_zero = sem("ws_zero"); ws_tr = sem("ws_tr"); wsel_ready = sem("wsel_ready"); qs_ready = sem("qs_ready")
        pidx_ready = sem("pidx_ready"); kx_in = [sem(f"kx_in{i}") for i in range(6)]
        kx_tr = sem("kx_tr"); kt_ev = sem("kt_ev"); kq_mm = sem("kq_mm")
        sc_relu = sem("sc_relu"); sc_row = sem("sc_row"); sc_out = sem("sc_out"); bm_ready = sem("bm_ready")
        kv_tr = sem("kv_tr"); kv_ev = sem("kv_ev"); qb_ready = sem("qb_ready")
        al_mm = sem("al_mm"); al_bias = sem("al_bias"); al_max = sem("al_max"); al_exp = sem("al_exp")
        p_ready = sem("p_ready"); at_tr = sem("at_tr"); at_ev = sem("at_ev"); av_mm = sem("av_mm"); av_mix = sem("av_mix")
        rot_done = sem("rot_done")
        kn_tr = sem("kn_tr"); kn_ev = sem("kn_ev"); sT_mm = sem("sT_mm"); am_ready = sem("am_ready")
        vn_tr = sem("vn_tr"); vn_ev = sem("vn_ev"); vx_ready = sem("vx_ready"); u_mm = sem("u_mm"); s_ready = sem("s_ready")
        us_mm = sem("us_mm"); sn_ready = sem("sn_ready"); sp_in = sem("sp_in"); ro_mm = sem("ro_mm"); ro_stat = sem("ro_stat")
        ro_nrm = sem("ro_nrm"); os_ev = sem("os_ev"); rn_tr = sem("rn_tr"); rn_mix = sem("rn_mix"); ros_mm = sem("ros_mm")
        st_s_out = sem("st_s_out"); st_p_out = sem("st_p_out")
        gs_tr = sem("gs_tr"); gs_n = sem("gs_n")
        l1_done = sem("l1_done"); bn_done = sem("bn_done"); brow_ready = sem("brow_ready"); cand_in = sem("cand_in"); tab_out = sem("tab_out")
        s_pti = sem("s_pti"); sel_f = sem("sel_f"); sel_tr = sem("sel_tr"); posu_ready = sem("posu_ready")
        rowf_in = sem("rowf_in"); row_ready = sem("row_ready"); nkb_in = [sem("new_keys_in"), sem("new_values_in")]
        kg_in = sem("kg_in"); vg_in = sem("vg_in")
        kg_fix = sem("kg_fix"); vg_fix = sem("vg_fix"); sk_tr = sem("sk_tr"); sk_ev = sem("sk_ev"); sl_mm = sem("sl_mm")
        sl_max = sem("sl_max"); sl_exp = sem("sl_exp"); sp_ready = sem("sp_ready"); spt_tr = sem("spt_tr"); spt_ev = sem("spt_ev")
        so_mm = sem("so_mm"); so_mix = sem("so_mix"); m_hi = sem("m_hi"); m_lo = sem("m_lo_even"); m_lo2 = sem("m_lo_odd")
        y_res = sem("y_res"); y_tr = sem("y_tr"); y_add = sem("y_add"); y_sq = sem("y_sq"); y_gain = sem("y_gain"); y_rs = sem("y_rs")
        fin_act = sem("fin_act"); fin_dve = sem("fin_dve")

        wiv = w_in[0].rearrange("(k p) c -> p k c", p=P)
        wov = w_out[0].rearrange("(k p) c -> p k c", p=P)

        def pieces(n):
            if n == 0:
                return [(0, 8704, 144)]
            if n <= 8:
                return [(0, 6656 + 256 * (n - 1), 256)]
            if n <= 10:
                return [(0, 5120 + 256 * (n - 9), 256)]
            if n <= 18:
                j = (n - 11) // 2
                return [(0, (4096 if n % 2 else 5632) + 256 * j, 256)]
            if n < NB_IN:
                h = (n - 19) // 2
                a, b = (1024, 0) if n % 2 else (2048, 3072)
                return [(0, a + P * h, P), (P, b + P * h, P)]
            return [(0, 256 * (n - NB_IN), 256)]

        class Step:
            def __init__(self, eng, n, *values):
                self.known = {v: eng.snap(v[0] * n + v[1]) for v in values}

            def __call__(self, x, c):
                return self.known[x, c]

        class Known:
            def __init__(self, n):
                self.n = n

            def __call__(self, x, c):
                return x * self.n + c

        def landed(n):
            return 16 * sum(len(pieces(i)) for i in range(n + 1))

        def ktile(n, a, k):
            return KC * (a if n < NB_IN else 1 - a) + k

        def banks(n):
            return (0, 2, 1, 3) if n in (0, NB - 1) else (0, 1, 2, 3)

        def width(n):
            return 144 if n == 0 else 256

        def tile_cols(n, t):
            return slice(16, 144) if n == 0 and t else slice(P * t, P * t + P)

        def tok(i):
            return slice(P * i, P * i + P) if i < QT else slice(T, NT)

        def rows(i):
            return P if i < QT else NS

        block = ctx.enter_context(nc.Block())

        @block.sync
        def _(sp):
            stores = [0]

            def store(dst, src, s=None):
                sp.dma_start(dst, src).then_inc(s or st_out, 16)
                if s is None:
                    stores[0] += 16

            def weights(n, a, step=None):
                v = step or Known(n)
                if n >= 1:
                    sp.wait_ge(w_lo, v(2, a - 1))
                src = wiv if n < NB_IN else wov
                k0 = ktile(n, a, 0)
                for dst, c, m in pieces(n):
                    columns = slice(c, c + m) if step is None else bass.ds(v(256, c - 256 * n), m)
                    sp.dma_start(Wraw[:, a, :, dst:dst + m], src[:, k0:k0 + KC, columns]).then_inc(w_in_sem[a], 16)

            def weight_loop(first, end):
                c = pieces(first)[0][1] - 256 * first
                with sp.Fori(first, end) as n:
                    step = Step(sp, n, (2, -1), (2, 0), (256, c))
                    weights(first, 0, step)
                    weights(first, 1, step)

            sp.dma_start(ident[:, :], c_ident).then_inc(s_ident, 16)
            sp.dma_start(gn[0:KT, :], norm_g[0].rearrange("(k p) -> k p", p=P)).then_inc(s_gin, 16)
            sp.dma_start(gn[KT:KT + NH, :], ret_norm_g[0]).then_inc(s_gin, 16)
            weights(0, 0)
            weights(0, 1)
            sp.dma_start(rot[:, :, :], c_rot).then_inc(s_const, 16)
            sp.dma_start(ctri[:, :], c_bias).then_inc(s_const, 16)
            sp.dma_start(tri[:, :], c_tri).then_inc(s_const, 16)
            sp.dma_start(cols[:, :, :], c_cols).then_inc(s_const, 16)
            sp.dma_start(eye[:, :], c_eye).then_inc(s_const, 16)
            for s in range(SEC):
                sp.dma_start(pti[NS * s:NS * s + NS, :], page_table[:, SPG * s:SPG * s + SPG]).then_inc(s_pti, 16)
            weights(1, 0)
            weights(1, 1)
            weight_loop(2, 9)
            weights(9, 0)
            weights(9, 1)
            sp.wait_ge(ki_ev, 4)
            store(nki_p[0, 0].rearrange("(t p) d -> p t d", p=P), kin[:, 0:QT, :])
            store(nki_s[0].rearrange("b o d -> b (o d)"), kin[0:NS, QT, :])
            weights(10, 0)
            weights(10, 1)
            for n in range(11, 13):
                weights(n, 0)
                weights(n, 1)
            sp.wait_ge(kv_ev, 8)
            store(nk_p[0, 0].rearrange("(t p) c d -> p t (c d)", p=P), kan[:, 0:QT, :])
            store(nk_s[0].rearrange("b o c d -> b (o c d)"), kan[0:NS, QT, :])
            store(nv_p[0, 0].rearrange("(t p) c d -> p t (c d)", p=P), van[:, 0:QT, :])
            store(nv_s[0].rearrange("b o c d -> b (o c d)"), van[0:NS, QT, :])
            for n in range(13, 17):
                weights(n, 0)
                weights(n, 1)
            sp.wait_ge(l1_done, 1)
            for s in range(SEC):
                sp.dma_start(cand[:, SELS * s:SELS * s + SELS], best[NS * s:NS * s + NS, :]).then_inc(cand_in, 16)
            sp.wait_ge(brow_ready, 1)
            for s in range(SEC):
                sp.dma_start(tabv[s], brow[NS * s:NS * s + NS, :]).then_inc(tab_out, 16)
            for n in range(17, 19):
                weights(n, 0)
                weights(n, 1)
            sp.wait_ge(st_out, stores[0])
            for n in (19, 20):
                weights(n, 0)
                weights(n, 1)

            def new_values(j):
                sp.dma_start(nkb[:, 1, :, :].rearrange("p b c -> p (b c)"),
                             nv_s[0, 2 * j:2 * j + 2].rearrange("b o c d -> (b o c d)").partition_broadcast(P)
                             ).then_inc(nkb_in[1], 16)

            old_states = lambda h: sp.dma_start(sp_[:, :, :], state_ret[0, :, h].rearrange("b d e -> d b e"))
            for h in range(NH):
                n = 21 + 2 * h
                weights(n, 0)
                weights(n, 1)
                if h == 0:
                    sp.wait_ge(av_mix, NH)
                    old_states(0).then_inc(sp_in, 16)
                weights(n + 1, 0)
                weights(n + 1, 1)
                sp.wait_ge(s_ready, 4 * h + 4)
                store(st_p[0, 0, h], stt[:, 3, :], st_p_out)
                sp.wait_ge(sn_ready, 2 * h + 2)
                store(st_s[0, :, h].rearrange("b d e -> d b e"), sp_[:, :, :], st_s_out)
                if h == HP:
                    sp.wait_ge(row_ready, 1)
                if h < NH - 1:
                    sp.wait_ge(ros_mm, h + 1)
                    sp.wait_ge(st_s_out, 16 * h + 16)
                    old_states(h + 1).then_inc(sp_in, 16)
                if 0 <= h - HP < 4:
                    if h > HP:
                        sp.wait_ge(vg_fix, h - HP)
                    new_values(h - HP)
            sp.wait_ge(st_s_out, 16 * NH)
            sp.wait_ge(st_p_out, 16 * NH)
            sp.wait_ge(gs_n, 2)
            sp.wait_ge(m_lo, KC)
            sp.wait_ge(m_lo2, KC)
            sp.dma_start(Y[:, :, :], x_prompt[0].rearrange("(t p) m -> p t m", p=P)).then_inc(y_res, 16)
            sp.dma_start(Ys[:, :], x_sample.rearrange("b o m -> (b o) m")).then_inc(y_res, 16)
            sp.dma_start(gfb[:, :], final_norm_g.partition_broadcast(P)).then_inc(y_res, 16)
            weight_loop(NB_IN + 2, NB)
            for i, by_act, by_dve in ((0, 1, 1), (1, 1, 3), (2, 2, 4), (3, 2, 6)):
                sp.wait_ge(fin_act, by_act)
                sp.wait_ge(fin_dve, by_dve)
                store(y_prompt[0, P * i:P * i + P, :], Y[:, i, :])
            sp.wait_ge(fin_dve, 7)
            store(y_sample.rearrange("b o m -> (b o) m"), Ys[:, :])
            sp.wait_ge(st_out, stores[0])
            sp.wait_ge(st_p_out, 16 * NH)
            sp.wait_ge(st_s_out, 16 * NH)

        @block.scalar
        def _(act):
            chain = [0]

            def link(ins):
                chain[0] += 1
                ins.then_inc(ach, 1)
                act.wait_ge(ach, chain[0])

            def hi(n, a, step=None):
                v = step or Known(n - 1)
                act.wait_ge(w_in_sem[a], v(16, landed(n) - 16 * (n - 1)))
                if n >= 1:
                    act.wait_ge(a_used, v(1, 1)) if a == 0 else act.wait_ge(acc_done, v(4, 4))
                nc.scalar.activation(Wh[:, a, :, 0:width(n)], Wraw[:, a, :, 0:width(n)], ACT.Copy).then_inc(w_hi, 1)

            def index_queries(step):
                for i in range(4):
                    t, half = i // 2, i % 2
                    act.wait_ge(acc_done, step(4, i + 1))
                    nc.scalar.activation(mix[:, bass.ds(step(2, t - 2), 1), HALF * half:HALF * half + HALF],
                                         bank[i][:, 0:HALF].unsqueeze(1), ACT.Copy).then_inc(acc_free, 1)

            def output_columns(step):
                for i in range(4):
                    t, half = i // 2, i % 2
                    act.wait_ge(acc_done, step(4, i + 1))
                    if i == 0:
                        act.wait_ge(y_tr, step(3, -3 * NB_IN))
                    nc.scalar.activation(yT[:, t, HALF * half:HALF * half + HALF], bank[i][:, 0:HALF],
                                         ACT.Copy).then_inc(acc_free, 1)

            def evacuate(n, which=range(4)):
                for place_ in which:
                    i = banks(n)[place_]
                    t, half = i // 2, i % 2
                    src = bank[i][:, 0:HALF]
                    s = slice(HALF * half, HALF * half + HALF)
                    act.wait_ge(acc_done, 4 * n + place_ + 1)
                    if n == 0:
                        ins = nc.scalar.activation((kiT if t == 0 else wiT)[:, s], src, ACT.Copy)
                    elif n <= 8:
                        ins = nc.scalar.activation(mix[:, 2 * (n - 1) + t, s], src, ACT.Copy)
                    elif n <= 10:
                        ins = nc.scalar.activation((kaT if n == 9 else vaT)[:, t, s], src, ACT.Copy)
                    elif n <= 18:
                        j = (n - 11) // 2
                        if n % 2:
                            ins = nc.scalar.activation(mix[:, 2 * j + t, s], src, ACT.Copy)
                        else:
                            ins = nc.scalar.activation(mix[:, NH + 2 * j + t, s], src, ACT.Silu)
                    elif n < NB_IN:
                        h = (n - 19) // 2
                        if n % 2:
                            if i == 0 and h:
                                act.wait_ge(us_mm, 2 * h)
                                act.wait_ge(rot_done, 2 * h)
                            nc.scalar.activation(XS[:, t, s], src, ACT.Copy)
                            nc.scalar.activation(XW[0:64, t, s], bank[i][64:P, 0:HALF], ACT.Copy)
                            ins = nc.scalar.activation(XW[64:P, t, s], bank[i][0:64, 0:HALF], ACT.Copy)
                        elif t == 0:
                            if i == 0 and h:
                                act.wait_ge(vn_tr, 2 * h)
                            ins = nc.scalar.activation(vT[:, s], src, ACT.Copy)
                        else:
                            ins = nc.scalar.activation(mix[:, h, s], src, ACT.Silu)
                    else:
                        if place_ == 0 and n > NB_IN:
                            act.wait_ge(y_tr, 3 * (n - NB_IN))
                        ins = nc.scalar.activation(yT[:, t, s], src, ACT.Copy)
                    ins.then_inc(acc_free, 1)

            def squares(i):
                act.wait_ge(x_in[i], 16)
                r = rows(i)
                if i == QT:
                    act.wait_ge(st4_set, 1)
                if i:
                    act.wait_ge(x_sq, i)
                nc.scalar.activation(mix[0:r, 0:4, 0:T], XT[0:r, i, :], ACT.Square,
                                     accum_out=st4[0:r, i:i + 1]).then_inc(x_sq, 1)

            for i in range(QT):
                act.dma_start(XT[:, i, :], x_prompt[0, P * i:P * i + P, :]).then_inc(x_in[i], 16)
            act.dma_start(XT[0:NS, QT, :], x_sample.rearrange("b o m -> (b o) m")).then_inc(x_in[QT], 16)
            act.dma_start(ptb[:, :, :].rearrange("p b j -> p (b j)"),
                          page_table.rearrange("b j -> (b j)").partition_broadcast(P)).then_inc(s_ptab, 16)
            squares(0)
            squares(1)
            squares(2)
            for i in range(5):
                for g in range(4):
                    v = 4 * i + g
                    act.wait_ge(x_g, v + 1)
                    nc.scalar.activation(Hh[:, 4 * g:4 * g + 4, tok(i)], HT[:, v % 4, :, 0:rows(i)],
                                         ACT.Copy).then_inc(h_hi, 1)
                if i == 0:
                    squares(3)
                    squares(4)
                if i == 1:
                    hi(0, 0)
                    hi(0, 1)
            for n in range(2):
                hi(n + 1, 0)
                evacuate(n)
                hi(n + 1, 1)
            with act.Fori(2, 9) as n:
                step = Step(act, n, (16, landed(3) - 32), (1, 1), (4, 1), (4, 2), (4, 3), (4, 4), (2, -2), (2, -1))
                hi(3, 0, step)
                index_queries(step)
                hi(3, 1, step)

            act.wait_ge(ki_tr, 1)
            nc.scalar.activation(kin[:, 0:QT, :].rearrange("p t d -> p (t d)"), bank[4][:, :], ACT.Copy).then_inc(ki_ev, 1)
            act.wait_ge(ki_tr, 2)
            nc.scalar.activation(kin[0:NS, QT, :], bank[5][0:NS, 0:P], ACT.Copy).then_inc(ki_ev, 1)
            act.wait_ge(ki_tr, 3)
            nc.scalar.activation(wn[:, 0:QT, :], bank[6][:, :].rearrange("p (t c) -> p t c", t=QT)[:, :, 112:P],
                                 ACT.Copy, scale=NIH ** -0.5 * SCALE).then_inc(ki_ev, 1)
            act.wait_ge(ki_tr, 4)
            nc.scalar.activation(wn[0:NS, QT, :], bank[7][0:NS, 112:P], ACT.Copy,
                                 scale=NIH ** -0.5 * SCALE).then_inc(ki_ev, 1)
            act.wait_ge(st_out, 32)
            i = 0
            for t in range(1, QT):
                for h in range(NIH):
                    w = P * (t + 1)
                    act.wait_ge(si_mm, i + 1)
                    if i >= 2:
                        act.wait_ge(si_acc, i - 1)
                    nc.scalar.activation(relu[:, i % 2, 0:w], bank[4 + i % 4][:, 0:w], ACT.Relu).then_inc(si_relu, 1)
                    i += 1
            n_si = i
            act.wait_ge(ws_tr, 1)
            act.wait_ge(ws_zero, 1)
            nc.scalar.activation(wsel[:, :, :].rearrange("p g (s x) -> p g s x", s=SEC)[:, :, :, 0:NS],
                                 bank[0][:, 0:2 * NS].rearrange("p (g b) -> p g b", g=2).unsqueeze(2).to_broadcast([P, 2, SEC, NS]),
                                 ACT.Copy).then_inc(wsel_ready, 1)
            act.wait_ge(si_acc, n_si)

            def keys_out(u):
                act.wait_ge(kx_tr, u + 1)
                if u >= 6:
                    act.wait_ge(kq_mm, (u - 6) // 4 + 1)
                nc.scalar.activation(kT[:, u % 6, :], bank[3 + u % 3][:, :], ACT.Copy).then_inc(kt_ev, 1)

            def relu_group(G):
                act.wait_ge(kq_mm, G + 1)
                if G >= 2:
                    act.wait_ge(sc_row, G - 1)
                w = T if G < 16 else 2
                nc.scalar.activation((wiT, relu2)[G % 2][:, 0:w], bank[6 + G % 2][:, 0:w], ACT.Relu).then_inc(sc_relu, 1)

            for u in range(4):
                keys_out(u)
            for G in range(16):
                for u in range(4 * G + 4, 4 * G + 7):
                    if u < 64:
                        keys_out(u)
                relu_group(G)
                if G < 15:
                    keys_out(4 * G + 7)
            relu_group(16)
            act.wait_ge(sc_row, 17)
            for half in range(2):
                nc.scalar.activation(scores[:, 0:SKEY].rearrange("b (p h q) -> b h q p", h=2, q=KPR // 2)[:, half],
                                     bank[half][32 * half:32 * half + NS * SEC, 0:T].rearrange("b (q p) -> b q p", q=KPR // 2),
                                     ACT.Copy).then_inc(sc_out, 1)
            nc.scalar.activation(scores[:, SKEY:SKEY + 1], bank[2][0:NS * SEC, 0:1], ACT.Identity,
                                 bias=cols[0:NS * SEC, 6, 0:1]).then_inc(sc_out, 1)

            for n in (9, 10):
                hi(n + 1, 0)
                if n == 9:
                    act.wait_ge(sc_out, 3)
                evacuate(n)
                hi(n + 1, 1)
            for m in range(4):
                dst = kan if m < 2 else van
                c = slice(P * (m % 2), P * (m % 2) + P)
                act.wait_ge(kv_tr, 2 * m + 1)
                nc.scalar.activation(dst[:, 0:QT, c], bank[4 + m % 2][:, :].rearrange("p (t d) -> p t d", t=QT),
                                     ACT.Copy).then_inc(kv_ev, 1)
                act.wait_ge(kv_tr, 2 * m + 2)
                nc.scalar.activation(dst[0:NS, QT, c], bank[6 + m % 2][0:NS, 0:P], ACT.Copy).then_inc(kv_ev, 1)

            def exps(h):
                for j, t in enumerate((2, 0, 1, 3)):
                    act.wait_ge(al_max, 4 * h + j + 1)
                    r = pb[:, SEG[t]:SEG[t] + P * (t + 1)]
                    nc.scalar.activation(r, r, ACT.Exp, bias=st4[:, 8 + t:9 + t],
                                         accum_out=st4[:, 12 + t:13 + t]).then_inc(al_exp, 1)

            def turned(h):
                if h:
                    act.wait_ge(av_mm, h)
                for j, (a, w) in enumerate(((0, 512), (512, 256), (768, 512))):
                    act.wait_ge(at_tr, 3 * h + j + 1)
                    nc.scalar.activation(pT[:, a:a + w], bank[4 + j][:, 0:w], ACT.Copy).then_inc(at_ev, 1)

            def attention(beta):
                h, what = (beta - 24) // 2, beta % 2
                if beta >= 24:
                    exps(h) if what == 0 else turned(h)

            for n in range(11, 19):
                hi(n + 1, 0)
                attention(2 * n)
                evacuate(n)
                hi(n + 1, 1)
                attention(2 * n + 1)
            def normalise(h):
                for c in range(4):
                    act.wait_ge(ro_stat, 4 * h + 4)
                    nc.scalar.activation(nrm[:, c, :], bank[4][:, P * c:P * c + P], ACT.Identity,
                                         bias=st4[:, 24 + c:25 + c], scale=st4[:, 20 + c:21 + c]).then_inc(ro_nrm, 1)
                act.wait_ge(ros_mm, h + 1)
                nc.scalar.activation(OS[:, h, :], bank[5][:, 0:NS], ACT.Copy).then_inc(os_ev, 1)

            act.wait_ge(st_out, 96)
            for h in range(NH):
                n = 19 + 2 * h
                hi(n + 1, 0)
                if h == 0:
                    exps(7)
                if 0 < h - HP <= 4:
                    for i in range(2):
                        act.wait_ge(sk_tr, 2 * (h - HP - 1) + i + 1)
                        nc.scalar.activation(skT[:, i, :], bank[7 - i][:, :], ACT.Copy).then_inc(sk_ev, 1)
                if h:
                    normalise(h - 1)
                evacuate(n)
                hi(n + 1, 1)
                if h == 0:
                    turned(7)
                if 0 < h - HP <= 4:
                    act.wait_ge(sl_max, h - HP)
                    nc.scalar.activation(sprob[:, :], sprob[:, :], ACT.Exp, bias=st4[0:16, 33:34],
                                         accum_out=st4[0:16, 34:35]).then_inc(sl_exp, 1)
                hi(n + 2, 0)
                act.wait_ge(kn_tr, 2 * h + 1)
                nc.scalar.activation(kn[:, :, :].rearrange("p c d -> p (c d)"), bank[4][:, :], ACT.Copy,
                                     scale=cols[:, 1, h:h + 1]).then_inc(kn_ev, 1)
                act.wait_ge(kn_tr, 2 * h + 2)
                nc.scalar.activation(kns[:, :], bank[5][0:NS, 0:P], ACT.Copy, scale=SCALE).then_inc(kn_ev, 1)
                if h == 0:
                    act.wait_ge(av_mix, NH)
                    act.wait_ge(qb_ready, 1)
                evacuate(n + 1)
                act.wait_ge(vn_tr, 2 * h + 1)
                nc.scalar.activation(vn[:, :, :].rearrange("p c d -> p (c d)"), bank[7][:, :], ACT.Copy).then_inc(vn_ev, 1)
                hi(n + 2, 1)

            def mix_high(k):
                nc.scalar.activation(Hh[:, k, :], mix[:, k, :], ACT.Copy).then_inc(m_hi, 1)

            act.wait_ge(acc_done, 4 * NB_IN)
            act.wait_ge(so_mix, 4)
            for k in range(KC, KT):
                mix_high(k)
            normalise(NH - 1)
            act.wait_ge(rn_mix, NH)
            act.wait_ge(gs_n, 2)
            for k in range(KC):
                mix_high(k)
            def y_squares(k, which=range(5), step=None):
                v = step or Known(k + NB_IN + 1)
                c, k_ = bass.ds(v(256, -256 * (NB_IN + 1)), 256), v(1, -NB_IN - 1)
                for i in which:
                    r = rows(i)
                    act.wait_ge(y_add, v(3, i // 2 + 1 - 3 * (NB_IN + 1)))
                    nc.scalar.activation(mix[0:r, 4 + i, 0:256], Y[:, i, c] if i < QT else Ys[:, c], ACT.Square,
                                         accum_out=ysq[0:r, i, bass.ds(k_, 1)]).then_inc(y_sq, 1)

            def y_scale(i):
                act.wait_ge(y_rs, i // 2 + 1)
                act.wait_ge(y_gain, 7)
                nc.scalar.activation(Y[:, i, 0:LASTC], Y[:, i, 0:LASTC], ACT.Copy, scale=st4[:, 40 + i:41 + i]).then_inc(fin_act, 1)

            hi(NB_IN + 1, 0)
            evacuate(NB_IN)
            hi(NB_IN + 1, 1)
            act.wait_ge(m_lo, KC)
            act.wait_ge(m_lo2, KC)
            with act.Fori(NB_IN + 1, NB - 1) as n:
                m = NB_IN + 1
                step = Step(act, n, (16, landed(m + 1) - 16 * m), (1, 1), (4, 1), (4, 2), (4, 3), (4, 4), (3, -3 * NB_IN),
                            (256, -256 * m), (1, -m), (3, 1 - 3 * m), (3, 2 - 3 * m), (3, 3 - 3 * m))
                hi(m + 1, 0, step)
                y_squares(0, step=step)
                output_columns(step)
                hi(m + 1, 1, step)
            y_squares(6)
            evacuate(NB - 1, (0, 1))
            evacuate(NB - 1, (2,))
            y_squares(7, (0, 1))
            y_scale(0)
            evacuate(NB - 1, (3,))
            y_squares(7, (2, 3, 4))
            y_scale(2)

        @block.gpsimd
        def _(pool):
            def lo(n, a, step=None):
                v = step or Known(n)
                pool.wait_ge(w_hi, v(2, a + 1))
                nc.gpsimd.tensor_tensor(Wl[:, a, :, :], Wraw[:, a, :, :], Wh[:, a, :, :].bitcast(F32),
                                        ALU.subtract).then_inc(w_lo, 1)

            def lo_loop(first, end):
                with pool.Fori(first, end) as n:
                    step = Step(pool, n, (2, 1), (2, 2))
                    lo(n, 0, step=step)
                    lo(n, 1, step=step)

            for i in range(5):
                for g in range(4):
                    v = 4 * i + g
                    pool.wait_ge(h_hi, v + 1)
                    nc.gpsimd.tensor_tensor(Hl[:, 4 * g:4 * g + 4, tok(i)], HT[:, v % 4, :, 0:rows(i)],
                                            Hh[:, 4 * g:4 * g + 4, tok(i)].bitcast(F32), ALU.subtract).then_inc(h_lo, 1)
            lo_loop(1, 10)
            cpages = cache_kidx[0].rearrange("n (r q) d -> (n r) (q d)", q=KPR)
            pool.wait_ge(pidx_ready, 1)
            for v in range(4 * 8):
                s, b = v // NS, v % NS
                if v >= 6:
                    w = v - 6
                    pool.wait_ge(kx_tr, 8 * (w // 4) + 4 + w % 4 + 1)
                nc.gpsimd.indirect_dma_start(
                    kx[v % 6][:, :], None, cpages,
                    bass.IndirectOffsetOnAxis(ap=pidx[:, b, s:s + 1], axis=0)).then_inc(kx_in[v % 6], 16)
            lo_loop(10, 19)
            kr = cache_k[0].rearrange("n s c d -> (n s) (c d)")
            vr = cache_v[0].rearrange("n s c d -> (n s) (c d)")

            def new_keys(j):
                nc.gpsimd.dma_start(nkb[:, 0, :, :].rearrange("p b c -> p (b c)"),
                                    nk_s[0, 2 * j:2 * j + 2].rearrange("b o c d -> (b o c d)").partition_broadcast(P)
                                    ).then_inc(nkb_in[0], 16)

            def selected(buf, rows_of, j, landed_):
                for i in range(2):
                    for half in range(2):
                        m = half * NS + 2 * j + i
                        nc.gpsimd.indirect_dma_start(buf[:, 2 * i + half, :], None, rows_of, bass.IndirectOffsetOnAxis(
                            ap=rowu[:, m:m + 1], axis=0)).then_inc(landed_, 16)

            def candidate_rows(which):
                for m in which:
                    nc.gpsimd.indirect_dma_start(rowf[:, m:m + 1], None, row_table, bass.IndirectOffsetOnAxis(
                        ap=posu[:, m:m + 1], axis=0)).then_inc(rowf_in, 16)

            def rotary(h, t):
                pool.wait_ge(acc_free, 4 * (19 + 2 * h) + 2 * t + 2)
                nc.gpsimd.tensor_tensor(XS[:, t, :], XS[:, t, :], rot[:, 0, :], ALU.mult).then_inc(pch, 1)
                nc.gpsimd.tensor_tensor(XW[:, t, :], XW[:, t, :], rot[:, 1, :], ALU.mult).then_inc(pch, 1)
                pool.wait_ge(pch, 4 * h + 2 * t + 2)
                if h and t == 0:
                    pool.wait_ge(sT_mm, h)
                if h and t == 1:
                    pool.wait_ge(ro_mm, h)
                    pool.wait_ge(ros_mm, h)
                nc.gpsimd.tensor_tensor(kq[:, t, :], XS[:, t, :], XW[:, t, :], ALU.add).then_inc(rot_done, 1)

            for h in range(NH):
                n = 19 + 2 * h
                lo(n, 0)
                if 0 < h - HP <= 4:
                    pool.wait_ge(row_ready, 1)
                    pool.wait_ge(sk_tr, 2 * (h - HP - 1))
                    if h - HP > 1:
                        pool.wait_ge(kg_fix, h - HP - 1)
                    new_keys(h - HP - 1)
                    selected(kg, kr, h - HP - 1, kg_in)
                lo(n, 1)
                lo(n + 1, 0)
                if h == HP:
                    pool.wait_ge(tab_out, 16 * SEC)
                    pool.wait_ge(posu_ready, 1)
                    candidate_rows(range(NS))
                rotary(h, 0)
                lo(n + 1, 1)
                rotary(h, 1)
                if h == HP:
                    candidate_rows(range(NS, 2 * NS))
                if 0 < h - HP <= 4:
                    pool.wait_ge(so_mm, h - HP - 1)
                    selected(vg, vr, h - HP - 1, vg_in)
            lo(35, 0)
            lo(35, 1)
            for i in range(0, KT, 2):
                k = ktile(NB_IN, i // KC, i % KC)
                pool.wait_ge(m_hi, i + 1)
                nc.gpsimd.tensor_tensor(Hl[:, k, :], mix[:, k, :], Hh[:, k, :].bitcast(F32), ALU.subtract).then_inc(m_lo, 1)

            def gain(v):
                c = bass.ds(v(256, -256 * 37), 256)
                pool.wait_ge(y_sq, v(5, 5 - 5 * 37))
                nc.gpsimd.tensor_tensor(Y[:, :, c], Y[:, :, c], gfb[:, c].unsqueeze(1).to_broadcast([P, QT, 256]),
                                        ALU.mult).then_inc(y_gain, 1)

            lo(36, 0)
            lo(36, 1)
            with pool.Fori(37, NB) as n:
                step = Step(pool, n, (2, 1), (2, 2), (256, -256 * 37), (5, 5 - 5 * 37))
                lo(n, 0, step=step)
                gain(step)
                lo(n, 1, step=step)
            gain(Known(43))
        @block.vector
        def _(dve):
            chain = [0]

            def link(ins):
                chain[0] += 1
                ins.then_inc(dch, 1)
                dve.wait_ge(dch, chain[0])

            v_ = nc.vector

            def rsqrt(x, done=None):
                r, w = x.shape
                y, z = rsq[0:r, 0, 0:w], rsq[0:r, 1, 0:w]
                link(v_.tensor_scalar(y.bitcast(I32), x.bitcast(I32), 1, None, ALU.arith_shift_right))
                link(v_.tensor_scalar(y.bitcast(I32), y.bitcast(I32), -1.0, float(0x5f3759df), ALU.mult, ALU.add))
                for step in range(3):
                    link(v_.tensor_tensor(z, y, y, ALU.mult))
                    link(v_.scalar_tensor_tensor(z, z, -0.5, x, ALU.mult, ALU.mult))
                    ins = v_.scalar_tensor_tensor(y if step < 2 else x, z, 1.5, y, ALU.add, ALU.mult)
                    if done and step == 2:
                        ins.then_inc(done, 1)
                    else:
                        link(ins)

            def norms(a, b):
                s = st4[:, a:b]
                dve.wait_ge(x_sq, b)
                link(v_.tensor_scalar(s, s, 1.0 / DM, EPS, ALU.mult, ALU.add))
                rsqrt(s)

            def scale(i):
                r = rows(i)
                v_.tensor_scalar(XT[0:r, i, :], XT[0:r, i, :], st4[0:r, i:i + 1], None, ALU.mult).then_inc(x_norm, 1)

            def gains(i):
                r = rows(i)
                for g in range(4):
                    v = 4 * i + g
                    dve.wait_ge(x_tr, v + 1)
                    if v >= 4:
                        dve.wait_ge(h_lo, v - 3)
                    v_.tensor_tensor(HT[:, v % 4, :, 0:r],
                                     bank[4 + v % 4][:, :].rearrange("p (k t) -> p k t", k=4)[:, :, 0:r],
                                     gin[:, 4 * g:4 * g + 4].unsqueeze(2).to_broadcast([P, 4, r]), ALU.mult).then_inc(x_g, 1)

            v_.memset(ysq[:, :, :], 0.0)
            v_.memset(st4[:, 4:5], 1.0).then_inc(st4_set, 1)
            norms(0, 2)
            scale(0)
            scale(1)
            dve.wait_ge(g_tr, 1)
            link(v_.tensor_copy(gains_T[:, :], bank[3][:, 0:KT + NH]))
            gains(0)
            norms(2, 3)
            scale(2)
            gains(1)
            norms(3, 5)
            scale(3)
            gains(2)
            for a in range(2):
                dve.wait_ge(w_hi, a + 1)
                w = width(0)
                v_.tensor_tensor(Wl[:, a, :, 0:w], Wraw[:, a, :, 0:w], Wh[:, a, :, 0:w].bitcast(F32),
                                 ALU.subtract).then_inc(w_lo, 1)
            scale(4)
            gains(3)
            gains(4)

            dve.wait_ge(s_const, 80)
            dve.wait_ge(s_ptab, 16)
            dve.wait_ge(h_lo, 20)
            link(v_.tensor_tensor(ptm[:, :, :], ptb[:, :, :].rearrange("p b (s j) -> p (b s) j", s=SEC),
                                  cols[:, 7, :].unsqueeze(1).to_broadcast([P, NS * SEC, SPG]), ALU.mult))
            link(v_.tensor_reduce(pidf[:, :, :].rearrange("p b s -> p (b s)"), ptm[:, :, :], AXX, ALU.add))
            v_.tensor_scalar(pidx[:, :, :], pidf[:, :, :], float(RPP), cols[:, 5, 0:1], ALU.mult, ALU.add).then_inc(pidx_ready, 1)
            v_.memset(wsel[:, :, :], 0.0).then_inc(ws_zero, 1)
            link(v_.memset(wsT[:, :, :, :], 0.0))
            link(v_.memset(QS[:, :], 0.0))
            dve.wait_ge(s_pti, 16 * SEC)
            v_.memset(ptf[:, SPG:SPG + 1], NEWROW)
            v_.tensor_scalar(ptf[:, 0:SPG], pti[:, :], float(P), None, ALU.mult)
            dve.wait_ge(acc_free, 4 * 9)
            v_.tensor_copy(QS[:, :].rearrange("p (b x) -> p b x", x=32)[:, :, 0:NIH],
                           mix[:, :, T:NT].rearrange("p h b -> p b h")).then_inc(qs_ready, 1)
            dve.wait_ge(ki_ev, 4)
            v_.tensor_tensor(wsT[:, :, :, 0:NIH], wn[0:NS, QT, :].unsqueeze(1).unsqueeze(1).to_broadcast([NS, 2, 4, NIH]),
                             eye[:, :].rearrange("b (g j) -> b g j", g=2).unsqueeze(3).to_broadcast([NS, 2, 4, NIH]),
                             ALU.mult).then_inc(ws_ready, 1)
            i = 0
            for t in range(1, QT):
                w = P * (t + 1)
                r = bm[:, SEG[t]:SEG[t] + w]
                for h in range(NIH):
                    dve.wait_ge(si_relu, i + 1)
                    if h:
                        dve.wait_ge(si_acc, i)
                        v_.scalar_tensor_tensor(r, relu[:, i % 2, 0:w], wn[:, t, h:h + 1], r, ALU.mult, ALU.add).then_inc(si_acc, 1)
                    else:
                        v_.tensor_scalar(r, relu[:, i % 2, 0:w], wn[:, t, h:h + 1], None, ALU.mult).then_inc(si_acc, 1)
                    i += 1
            dve.wait_ge(si_acc, i)
            for t in range(1, QT):
                e = bm[:, SEG[t] + P * t:SEG[t] + P * t + P]
                link(v_.tensor_tensor(e, e, ctri[:, :], ALU.add))
            for t in range(1, QT):
                r = bm[:, SEG[t]:SEG[t] + P * (t + 1)]
                for _ in range(SELP // 8):
                    link(v_.max(top8[:, :], r))
                    link(v_.match_replace(r, top8[:, :], r, TAKEN))
                link(v_.tensor_scalar(r, r, TAKEN / 2, NEG, ALU.is_gt, ALU.mult))
            v_.tensor_copy(bm[:, SEG[0]:SEG[0] + P], ctri[:, :]).then_inc(bm_ready, 1)

            L1 = 3 * SELS // 8
            ROWS = 4 + 2 * (SPG + 1)
            done = [0]

            def first_level(k):
                row, top = scores[:, 0:SKEY + 1], best[:, 8 * (k // 3):8 * (k // 3) + 8]
                if k == 0:
                    dve.wait_ge(sc_out, 3)
                if k % 3 == 0:
                    link(v_.max(top, row))
                elif k % 3 == 1:
                    link(v_.max_index(besti[:, 8 * (k // 3):8 * (k // 3) + 8], top, row))
                elif k < L1 - 1:
                    link(v_.match_replace(row, top, row, TAKEN))
                else:
                    v_.match_replace(row, top, row, TAKEN).then_inc(l1_done, 1)

            def candidate_rows(k):
                bits = bterm[:, :].bitcast(U32)
                if k == 0:
                    link(v_.tensor_scalar(bits, besti[:, :], 7, None, ALU.logical_shift_right))
                elif k == 1:
                    link(v_.tensor_copy(bpage[:, :], bits))
                elif k == 2:
                    link(v_.tensor_scalar(bits, besti[:, :], P - 1, None, ALU.bitwise_and))
                elif k == 3:
                    link(v_.tensor_copy(brow[:, :], bits))
                elif k % 2 == 0:
                    j = (k - 4) // 2
                    link(v_.tensor_scalar(bterm[:, :], bpage[:, :], float(j), ptf[:, j:j + 1], ALU.is_equal, ALU.mult))
                elif k < ROWS - 1:
                    link(v_.tensor_tensor(brow[:, :], brow[:, :], bterm[:, :], ALU.add))
                else:
                    v_.tensor_tensor(brow[:, :], brow[:, :], bterm[:, :], ALU.add).then_inc(brow_ready, 1)

            def second_level(k):
                top = top8[0:NS, :]
                if k == 0:
                    dve.wait_ge(cand_in, 16 * SEC)
                if k % 3 == 0:
                    link(v_.max(top, cand[:, :]))
                elif k % 3 == 1:
                    link(v_.max_index(besti[0:NS, 8 * (k // 3):8 * (k // 3) + 8], top, cand[:, :]))
                else:
                    link(v_.match_replace(cand[:, :], top, cand[:, :], TAKEN))

            def topk(m):
                for _ in range(m):
                    k = done[0]
                    done[0] += 1
                    if k < L1:
                        first_level(k)
                    elif k < L1 + ROWS:
                        candidate_rows(k - L1)
                    elif k < 2 * L1 + ROWS:
                        second_level(k - L1 - ROWS)
                    elif k == 2 * L1 + ROWS:
                        link(v_.tensor_copy(sidf[:, :], besti[0:NS, :]))
                        v_.tensor_scalar(sidf[:, :], sidf[:, :], cols[0:NS, 6, 1:2], None, ALU.add).then_inc(sel_f, 1)

            def logits(h):
                for j, (a, w) in enumerate(((0, 512), (512, 256), (768, 512))):
                    dve.wait_ge(al_mm, 3 * h + j + 1)
                    if h:
                        dve.wait_ge(at_tr, 3 * h)
                    v_.scalar_tensor_tensor(pb[:, a:a + w], bank[4 + j][:, 0:w], SCALE, bm[:, a:a + w],
                                            ALU.mult, ALU.add).then_inc(al_bias, 1)
                for j, t in enumerate((2, 0, 1, 3)):
                    dve.wait_ge(al_bias, 3 * h + (1, 1, 2, 3)[j])
                    link(v_.tensor_reduce(st4[:, 8 + t:9 + t], pb[:, SEG[t]:SEG[t] + P * (t + 1)], AXX, ALU.max))
                    v_.tensor_scalar(st4[:, 8 + t:9 + t], st4[:, 8 + t:9 + t], -1.0, None, ALU.mult).then_inc(al_max, 1)
                for j, t in enumerate((2, 0, 1, 3)):
                    dve.wait_ge(al_exp, 4 * h + j + 1)
                    link(v_.reciprocal(st4[:, 16 + t:17 + t], st4[:, 12 + t:13 + t]))
                    r = pb[:, SEG[t]:SEG[t] + P * (t + 1)]
                    v_.tensor_scalar(r, r, st4[:, 16 + t:17 + t], None, ALU.mult).then_inc(p_ready, 1)

            def gate(h):
                dve.wait_ge(av_mm, h + 1)
                dve.wait_ge(acc_free, 4 * (12 + 2 * (h // 2)) + 4)
                v_.tensor_tensor(mix[:, NH + h, 0:T], bank[7][:, :], mix[:, NH + h, 0:T], ALU.mult).then_inc(av_mix, 1)

            topk(56)
            for beta in range(24, 38):
                h = (beta - 24) // 2
                if beta % 2 == 0:
                    if h:
                        gate(h - 1)
                    logits(h)
                topk(8)
            gate(6)
            logits(7)
            link(v_.memset(QB[:, :], 0.0))
            v_.tensor_copy(QB[:, :].rearrange("p (b c x) -> p b c x", b=NS, c=NKV)[:, :, :, 0:NG],
                           mix[:, 0:NH, T:NT].rearrange("p (c g) b -> p b c g", c=NKV)).then_inc(qb_ready, 1)

            def stats(h):
                dve.wait_ge(ro_mm, h + 1)
                if h:
                    dve.wait_ge(ro_nrm, 4 * h)
                for c in range(4):
                    v_.bn_stats(bnst[:, c, :], bank[4][:, P * c:P * c + P]).then_inc(bn_done, 1)
                for c in range(4):
                    dve.wait_ge(bn_done, 8 * h + c + 1)
                    v_.bn_aggr(mv[:, c, :], bnst[:, c, :]).then_inc(bn_done, 1)
                dve.wait_ge(bn_done, 8 * h + 8)
                q = lambda a: st4[:, a:a + 4]
                link(v_.tensor_scalar(q(28), mv[:, :, 1], cols[:, 3, h:h + 1], EPS, ALU.mult, ALU.add))
                rsqrt(q(28))
                link(v_.tensor_scalar(q(20), q(28), cols[:, 2, h:h + 1], None, ALU.mult))
                v_.scalar_tensor_tensor(q(24), mv[:, :, 0], -1.0, q(20), ALU.mult, ALU.mult).then_inc(ro_stat, 4)

            def gated(h):
                dve.wait_ge(rn_tr, h + 1)
                v_.scalar_tensor_tensor(mix[:, h, 0:T], bank[6][:, :], gret[:, h:h + 1], mix[:, h, 0:T],
                                        ALU.mult, ALU.mult).then_inc(rn_mix, 1)

            def sample_gate(j):
                dve.wait_ge(so_mm, j + 1)
                s = slice(T + 2 * j, T + 2 * j + 2)
                v_.tensor_tensor(mix[:, NH:KT, s], bank[7][:, 32:48].rearrange("p (i h) -> p h i", i=2),
                                 mix[:, NH:KT, s], ALU.mult).then_inc(so_mix, 1)

            def new_token(what, j):
                buf, landed_, fixed = ((kg, kg_in, kg_fix), (vg, vg_in, vg_fix))[what]
                dve.wait_ge(landed_, 64 * (j + 1))
                dve.wait_ge(nkb_in[what], 16 * (j + 1))
                for i in range(2):
                    for half in range(2):
                        m = half * NS + 2 * j + i
                        ins = v_.copy_predicated(buf[:, 2 * i + half, :], isnew[:, m:m + 1].to_broadcast([P, 256]),
                                                 nkb[:, what, i, :])
                ins.then_inc(fixed, 1)

            def sample_softmax(j):
                dve.wait_ge(sl_mm, j + 1)
                link(v_.tensor_scalar(sprob[:, :], bank[7][0:16, 0:SELS], SCALE, None, ALU.mult))
                link(v_.tensor_reduce(st4[0:16, 33:34], sprob[:, :], AXX, ALU.max))
                v_.tensor_scalar(st4[0:16, 33:34], st4[0:16, 33:34], -1.0, None, ALU.mult).then_inc(sl_max, 1)
                dve.wait_ge(sl_exp, j + 1)
                link(v_.reciprocal(st4[0:16, 35:36], st4[0:16, 34:35]))
                v_.tensor_scalar(sprob[:, :], sprob[:, :], st4[0:16, 35:36], None, ALU.mult).then_inc(sp_ready, 1)

            for h in range(NH):
                if h:
                    stats(h - 1)
                if h == HP:
                    dve.wait_ge(sel_tr, 1)
                    v_.tensor_copy(posu[:, :], bank[7][:, 0:2 * NS]).then_inc(posu_ready, 1)
                topk(4)
                if h:
                    gated(h - 1)
                if h == 0:
                    topk(14)
                    gate(7)
                    topk(8)
                else:
                    topk(22)
                if h == HP + 5:
                    sample_gate(3)
                if 0 < h - HP <= 4:
                    sample_softmax(h - HP - 1)
                    dve.wait_ge(spt_tr, h - HP)
                    if h - HP > 1:
                        sample_gate(h - HP - 2)
                    v_.tensor_copy(spT[:, :, :].rearrange("p a b -> p (a b)"), bank[7][:, 0:32]).then_inc(spt_ev, 1)
                dve.wait_ge(vn_tr, 2 * h + 2)
                dve.wait_ge(rot_done, 2 * h + 2)
                v_.tensor_tensor(vx[:, :, :], bank[5][0:NS, 0:P].unsqueeze(1).to_broadcast([NS, NS, P]),
                                 eye[:, :].unsqueeze(2).to_broadcast([NS, NS, P]), ALU.mult).then_inc(vx_ready, 1)
                dve.wait_ge(sT_mm, h + 1)
                v_.scalar_tensor_tensor(am[:, :, :], bank[6][:, :].rearrange("p (c i) -> p c i", c=4), cols[:, 0, h:h + 1],
                                        tri[:, :].unsqueeze(1).to_broadcast([P, 4, P]), ALU.mult, ALU.mult).then_inc(am_ready, 1)
                dve.wait_ge(u_mm, h + 1)
                if h:
                    dve.wait_ge(st_p_out, 16 * h)
                v_.tensor_copy(stt[:, 0, :], bank[4][:, 0:P]).then_inc(s_ready, 1)
                for c in range(1, 4):
                    dve.wait_ge(s_ready, 4 * h + c)
                    v_.scalar_tensor_tensor(stt[:, c, :], stt[:, c - 1, :], cols[:, 4, h:h + 1],
                                            bank[4][:, P * c:P * c + P], ALU.mult, ALU.add).then_inc(s_ready, 1)
                dve.wait_ge(sp_in, 16 * (h + 1))
                for j in range(2):
                    dve.wait_ge(us_mm, 2 * h + j + 1)
                    r = sp_[:, 4 * j:4 * j + 4, :].rearrange("p b e -> p (b e)")
                    v_.scalar_tensor_tensor(r, r, float(1.0 - 2.0 ** (-5 - h)), bank[(5, 7)[j]][:, :],
                                            ALU.mult, ALU.add).then_inc(sn_ready, 1)
                topk(8 if h != HP - 1 else 6 * SELS)
                if h == HP:
                    dve.wait_ge(rowf_in, 16 * 2 * NS)
                    v_.tensor_scalar(isnew[:, :], rowf[:, :], NEWROW / 2, None, ALU.is_gt)
                    v_.tensor_scalar(rowu[:, :], rowf[:, :], float(cache_k.shape[1] * P - 1), None, ALU.min).then_inc(row_ready, 1)
                if 0 < h - HP <= 4:
                    new_token(1, h - HP - 1)
                if 0 <= h - HP < 4:
                    new_token(0, h - HP)
            def mix_low(half):
                for i in range(KC * half + 1, KC * half + KC, 2):
                    k = ktile(NB_IN, half, i % KC)
                    dve.wait_ge(m_hi, i + 1)
                    v_.tensor_tensor(Hl[:, k, :], mix[:, k, :], Hh[:, k, :].bitcast(F32), ALU.subtract).then_inc(m_lo2, 1)

            mix_low(0)
            stats(NH - 1)
            gated(NH - 1)
            dve.wait_ge(gs_tr, 1)
            link(v_.bn_stats(bnst[0:64, 0, :], bank[7][0:64, 0:P]))
            link(v_.bn_aggr(mv[0:64, 0, :], bnst[0:64, 0, :]))
            link(v_.tensor_scalar(st4[0:64, 28:29], mv[0:64, 0, 1:2], EPS, None, ALU.add))
            rsqrt(st4[0:64, 28:29])
            v_.tensor_scalar(nrm[0:64, 0, :], bank[7][0:64, 0:P], mv[0:64, 0, 0:1], st4[0:64, 28:29],
                             ALU.subtract, ALU.mult).then_inc(gs_n, 1)
            dve.wait_ge(gs_tr, 2)
            link(v_.tensor_tensor(nrm[:, 1, 0:64].rearrange("p (h b) -> p h b", h=NH),
                                  bank[7][:, 0:64].rearrange("p (h b) -> p h b", h=NH),
                                  gret[:, :].unsqueeze(2).to_broadcast([P, NH, NS]), ALU.mult))
            v_.tensor_tensor(mix[:, 0:NH, T:NT], nrm[:, 1, 0:64].rearrange("p (h b) -> p h b", h=NH),
                             mix[:, 0:NH, T:NT], ALU.mult).then_inc(gs_n, 1)
            mix_low(1)
            dve.wait_ge(y_res, 48)
            def y_block(v, which=range(3)):
                c = bass.ds(v(256, 0), 256)
                for j in which:
                    dve.wait_ge(y_tr, v(3, j + 1))
                    if j < 2:
                        r = Y[:, 2 * j:2 * j + 2, c]
                        ins = v_.tensor_tensor(r, r, bank[4 + j][:, :].rearrange("p (t m) -> p t m", t=2), ALU.add)
                    else:
                        ins = v_.tensor_tensor(Ys[:, c], Ys[:, c], bank[6][0:NS, 0:256], ALU.add)
                    ins.then_inc(y_add, 1)

            def y_rsqrt(a, b):
                s = st4[:, 40 + a:40 + b]
                link(v_.tensor_reduce(s, ysq[:, a:b, :], AXX, ALU.add))
                link(v_.tensor_scalar(s, s, 1.0 / DM, EPS, ALU.mult, ALU.add))
                rsqrt(s, y_rs)

            def last_block(i):
                r = Y[:, i, LASTC:DM]
                v_.scalar_tensor_tensor(r, r, st4[:, 40 + i:41 + i], gfb[:, LASTC:DM], ALU.mult, ALU.mult).then_inc(fin_dve, 1)

            def other_blocks(i):
                v_.tensor_scalar(Y[:, i, 0:LASTC], Y[:, i, 0:LASTC], st4[:, 40 + i:41 + i], None, ALU.mult).then_inc(fin_dve, 1)

            with dve.Fori(0, 7) as k:
                y_block(Step(dve, k, (256, 0), (3, 1), (3, 2), (3, 3)))
            y_block(Known(7), (0,))
            dve.wait_ge(y_sq, 37)
            y_rsqrt(0, 2)
            dve.wait_ge(y_rs, 1)
            last_block(0)
            last_block(1)
            dve.wait_ge(y_gain, 7)
            other_blocks(1)
            y_block(Known(7), (1, 2))
            dve.wait_ge(y_sq, 40)
            y_rsqrt(2, 5)
            dve.wait_ge(y_rs, 2)
            last_block(2)
            last_block(3)
            other_blocks(3)
            v_.scalar_tensor_tensor(Ys[:, :], Ys[:, :], st4[0:NS, 44:45], gfb[0:NS, :], ALU.mult, ALU.mult).then_inc(fin_dve, 1)

        @block.tensor
        def _(pe):
            mm = nc.tensor.matmul

            def part(n, a, i, step=None):
                v = step or Known(n)
                t, half = i // 2, i % 2
                s = slice(HALF * half, HALF * half + HALF)
                if a == 0 and n >= 1:
                    pe.wait_ge(acc_free, v(4, banks(n - 1).index(i) - 3))
                for k in range(KC):
                    kk = ktile(n, a, k)
                    if n == NB_IN and i == 0:
                        pe.wait_ge(m_lo2 if k % 2 else m_lo, (KC * a + k) // 2 + 1)
                    wh, wl = Wh[:, a, k, tile_cols(n, t)], Wl[:, a, k, tile_cols(n, t)]
                    mm(bank[i][:, 0:HALF], wh, Hh[:, kk, s], start=(a == 0 and k == 0), stop=False)
                    mm(bank[i][:, 0:HALF], wh, Hl[:, kk, s], start=False, stop=False)
                    last = mm(bank[i][:, 0:HALF], wl, Hh[:, kk, s], start=False, stop=(a == 1 and k == KC - 1))
                if a == 1:
                    last.then_inc(acc_done, 1)
                return last

            def chunk(n, a, between=None, step=None):
                pe.wait_ge(w_lo, (step or Known(n))(2, a + 1))
                for i in range(4):
                    if i == 2 and between:
                        between()
                    last = part(n, a, i, step)
                if a == 0:
                    last.then_inc(a_used, 1)

            def turn(out, in_, k=P):
                return nc.tensor.transpose(out, in_, ident[0:k, 0:k])

            pe.wait_ge(s_ident, 16)
            def turn_tokens(i):
                r = rows(i)
                pe.wait_ge(x_norm, i + 1)
                for g in range(4):
                    v = 4 * i + g
                    if v >= 4:
                        pe.wait_ge(x_g, v - 3)
                    for k in range(4):
                        c = P * (4 * g + k)
                        last = turn(bank[4 + v % 4][:, P * k:P * k + r], XT[0:r, i, c:c + P], r)
                    last.then_inc(x_tr, 1)

            pe.wait_ge(s_gin, 32)
            turn(bank[3][:, 0:KT + NH], gn[:, :], KT + NH).then_inc(g_tr, 1)
            for i in range(4):
                turn_tokens(i)
            pe.wait_ge(h_lo, 12)
            pe.wait_ge(w_lo, 2)
            part(0, 0, 0)
            part(0, 1, 0)
            turn_tokens(QT)
            part(0, 0, 2)
            part(0, 1, 2)
            pe.wait_ge(h_lo, 20)
            part(0, 0, 1)
            part(0, 0, 3).then_inc(a_used, 1)
            part(0, 1, 1)
            part(0, 1, 3)
            chunk(1, 0)
            chunk(1, 1)
            with pe.Fori(2, 9) as n:
                step = Step(pe, n, (2, 1), (2, 2), (4, -3), (4, -2), (4, -1), (4, 0))
                chunk(2, 0, step=step)
                chunk(2, 1, step=step)

            for q, src in ((0, kiT), (2, wiT)):
                for t in range(QT):
                    last = turn(bank[4 + q][:, P * t:P * t + P], src[:, tok(t)])
                last.then_inc(ki_tr, 1)
                turn(bank[5 + q][0:NS, 0:P], src[:, T:NT]).then_inc(ki_tr, 1)
            pe.wait_ge(ki_ev, 4)
            pe.wait_ge(acc_free, 36)
            i = 0
            for t in range(1, QT):
                for h in range(NIH):
                    w = P * (t + 1)
                    if i >= 4:
                        pe.wait_ge(si_relu, i - 3)
                    mm(bank[4 + i % 4][:, 0:w], mix[:, h, tok(t)], kiT[:, 0:w], start=True, stop=True).then_inc(si_mm, 1)
                    i += 1
            pe.wait_ge(ws_ready, 1)
            for g in range(2):
                last = turn(bank[0][:, NS * g:NS * g + NS], wsT[:, g, :, :].rearrange("a b h -> a (b h)"), NS)
            last.then_inc(ws_tr, 1)
            pe.wait_ge(si_relu, i)
            pe.wait_ge(qs_ready, 1)
            qs = QS[:, :].rearrange("p (b m) -> p b m", b=NS)

            def turn_keys(u):
                G, j = u // 4, u % 4
                v, half = 4 * (G // 2) + j, G % 2
                pe.wait_ge(kx_in[v % 6], 16 * (v // 6 + 1))
                if u >= 3:
                    pe.wait_ge(kt_ev, u - 2)
                for q in range(KPR // 2):
                    c = P * (KPR // 2 * half + q)
                    last = turn(bank[3 + u % 3][:, P * q:P * q + P], kx[v % 6][:, c:c + P])
                last.then_inc(kx_tr, 1)

            def products(G):
                pe.wait_ge(kt_ev, 4 * G + 4)
                if G >= 2:
                    pe.wait_ge(sc_relu, G - 1)
                for j in range(4):
                    last = mm(bank[6 + G % 2][32 * j:32 * j + 32, :], qs[:, 4 * (G // 2 % 2) + j, :], kT[:, (4 * G + j) % 6, :],
                              start=True, stop=True, tile_position=(0, 32 * j))
                last.then_inc(kq_mm, 1)

            def row_product(G):
                s, g, half = G // 4, G // 2 % 2, G % 2
                pe.wait_ge(sc_relu, G + 1)
                pe.wait_ge(wsel_ready, 1)
                mm(bank[half][32 * half:32 * half + NS * SEC, :], wsel[:, g, NS * SEC * s:NS * SEC * s + NS * SEC],
                   (wiT, relu2)[half][:, 0:T], start=(G < 2), stop=(G >= 14), tile_position=(0, 32 * half)).then_inc(sc_row, 1)

            for u in range(4):
                turn_keys(u)
            for G in range(16):
                for u in range(4 * G + 4, 4 * G + 7):
                    if u < 64:
                        turn_keys(u)
                products(G)
                if G and G % 2 == 0:
                    row_product(G - 2)
                    row_product(G - 1)
                if G < 15:
                    turn_keys(4 * G + 7)
            row_product(14)
            row_product(15)
            pe.wait_ge(sc_relu, 15)
            for g in range(2):
                for j in range(4):
                    b = 4 * g + j
                    last = mm(bank[6][32 * j:32 * j + 32, g:g + 1], qs[:, b, :], kiT[:, T + b:T + b + 1],
                              start=True, stop=True, tile_position=(0, 32 * j))
            last.then_inc(kq_mm, 1)
            pe.wait_ge(sc_relu, 17)
            for g in range(2):
                last = mm(bank[2][0:NS * SEC, 0:1], wsel[:, g, NS * SEC * 3:NS * SEC * 4], wiT[:, g:g + 1],
                          start=(g == 0), stop=(g == 1))
            last.then_inc(sc_row, 1)
            pe.wait_ge(sc_out, 3)

            for n in (9, 10):
                chunk(n, 0)
                chunk(n, 1)
            pe.wait_ge(acc_free, 44)
            for m in range(4):
                src = (kaT if m < 2 else vaT)[:, m % 2, :]
                if m >= 2:
                    pe.wait_ge(kv_ev, 2 * m - 2)
                for t in range(QT):
                    last = turn(bank[4 + m % 2][:, P * t:P * t + P], src[:, tok(t)])
                last.then_inc(kv_tr, 1)
                turn(bank[6 + m % 2][0:NS, 0:P], src[:, T:NT]).then_inc(kv_tr, 1)

            def query_key(h):
                pe.wait_ge(bm_ready, 1)
                pe.wait_ge(acc_free, 4 * (11 + 2 * (h // 2)) + 4)
                if h == 0:
                    pe.wait_ge(kv_ev, 8)
                else:
                    pe.wait_ge(at_ev, 3 * h)
                for t, bk, o_ in ((2, 4, 0), (0, 4, 384), (1, 5, 0), (3, 6, 0)):
                    w = P * (t + 1)
                    last = mm(bank[bk][:, o_:o_ + w], mix[:, h, tok(t)], kaT[:, h // NG, 0:w], start=True, stop=True)
                    if t != 2:
                        last.then_inc(al_mm, 1)

            def turn_probs(h):
                pe.wait_ge(p_ready, 4 * h + 4)
                for bk, a, w in ((4, 0, 512), (5, 512, 256), (6, 768, 512)):
                    for k in range(w // P):
                        last = turn(bank[bk][:, P * k:P * k + P], pb[:, a + P * k:a + P * k + P])
                    last.then_inc(at_tr, 1)

            def prob_value(h):
                pe.wait_ge(at_ev, 3 * h + 3)
                if h:
                    pe.wait_ge(av_mix, h)
                c = P * (h // NG)
                for t in range(QT):
                    for s in range(t + 1):
                        last = mm(bank[7][:, P * t:P * t + P], van[:, s, c:c + P],
                                  pT[:, SEG[t] + P * s:SEG[t] + P * s + P], start=(s == 0), stop=(s == t))
                last.then_inc(av_mm, 1)

            for n in range(11, 19):
                for a in range(2):
                    chunk(n, a)
                    beta = 2 * n + a
                    if beta >= 24:
                        h = (beta - 24) // 2
                        if beta % 2 == 0:
                            if h:
                                prob_value(h - 1)
                            query_key(h)
                        else:
                            turn_probs(h)
            def outputs(h):
                pe.wait_ge(am_ready, h + 1)
                pe.wait_ge(s_ready, 4 * h + 4)
                for c in range(4):
                    o_ = bank[4][:, P * c:P * c + P]
                    last = mm(o_, am[:, c, :], vn[:, c, :], start=True, stop=(c == 0))
                    if c:
                        last = mm(o_, kq[:, 1, tok(c)], stt[:, c - 1, :], start=False, stop=True)
                last.then_inc(ro_mm, 1)
                pe.wait_ge(sn_ready, 2 * h + 2)
                for b in range(NS):
                    last = mm(bank[5][:, b:b + 1], sp_[:, b, :], kq[:, 1, T + b:T + b + 1], start=True, stop=True)
                last.then_inc(ros_mm, 1)

            def turn_selected(j):
                pe.wait_ge(kg_fix, j + 1)
                for i in range(2):
                    for c in range(NKV):
                        for half in range(2):
                            k = 2 * c + half
                            last = turn(bank[7 - i][:, P * k:P * k + P], kg[:, 2 * i + half, P * c:P * c + P])
                    last.then_inc(sk_tr, 1)

            def sample_logits(j):
                pe.wait_ge(qb_ready, 1)
                pe.wait_ge(sk_ev, 2 * j + 2)
                for m in range(4):
                    last = mm(bank[7][0:16, 0:SELS], QB[:, 80 * j + 16 * m:80 * j + 16 * m + 16],
                              skT[:, m // 2, SELS * (m % 2):SELS * (m % 2) + SELS], start=(m == 0), stop=(m == 3))
                last.then_inc(sl_mm, 1)

            def turn_sample_probs(j):
                for half in range(2):
                    last = turn(bank[7][:, 16 * half:16 * half + 16], sprob[:, P * half:P * half + P], 16)
                last.then_inc(spt_tr, 1)

            def sample_value(j):
                pe.wait_ge(spt_ev, j + 1)
                pe.wait_ge(vg_fix, j + 1)
                for m in range(4):
                    i, c = m // 2, m % 2
                    for half in range(2):
                        last = mm(bank[7][:, 32 + NG * m:32 + NG * m + NG], vg[:, 2 * i + half, P * c:P * c + P],
                                  spT[:, half, NG * m:NG * m + NG], start=(half == 0), stop=(half == 1))
                last.then_inc(so_mm, 1)

            def turn_outputs(h):
                pe.wait_ge(ro_nrm, 4 * h + 4)
                pe.wait_ge(am_ready, h + 1)
                if 0 <= h - HP < 4:
                    pe.wait_ge(sk_ev, 2 * (h - HP) + 2)
                for c in range(4):
                    last = turn(bank[6][:, P * c:P * c + P], nrm[:, c, :])
                last.then_inc(rn_tr, 1)

            for h in range(NH):
                n = 19 + 2 * h
                chunk(n, 0)
                if h:
                    outputs(h - 1)
                else:
                    prob_value(6)
                    query_key(7)
                if h == HP:
                    pe.wait_ge(sel_f, 1)
                    for half in range(2):
                        last = turn(bank[7][:, NS * half:NS * half + NS], sidf[:, P * half:P * half + P], NS)
                    last.then_inc(sel_tr, 1)
                if 0 < h - HP <= 4:
                    turn_selected(h - HP - 1)
                chunk(n, 1)
                if h:
                    turn_outputs(h - 1)
                else:
                    turn_probs(7)
                if 0 < h - HP <= 4:
                    sample_logits(h - HP - 1)
                chunk(n + 1, 0)
                if h == 0:
                    prob_value(7)
                if 0 < h - HP <= 4:
                    pe.wait_ge(sp_ready, h - HP)
                if 1 < h - HP <= 5:
                    sample_value(h - HP - 2)
                if 0 < h - HP <= 4:
                    turn_sample_probs(h - HP - 1)
                pe.wait_ge(rot_done, 2 * h + 1)
                if h:
                    pe.wait_ge(os_ev, h)
                for c in range(4):
                    last = turn(bank[4][:, P * c:P * c + P], kq[:, 0, tok(c)])
                last.then_inc(kn_tr, 1)
                turn(bank[5][0:NS, 0:P], kq[:, 0, T:NT]).then_inc(kn_tr, 1)
                chunk(n + 1, 1)
                pe.wait_ge(acc_free, 4 * (n + 1) + 2)
                pe.wait_ge(kn_ev, 2 * h + 2)
                pe.wait_ge(sn_ready, 2 * h) if h else pe.wait_ge(av_mix, NH)
                if h == HP:
                    pe.wait_ge(posu_ready, 1)
                if 0 < h - HP <= 4:
                    pe.wait_ge(spt_ev, h - HP)
                if h == HP + 5:
                    pe.wait_ge(so_mix, 4)
                for c in range(4):
                    last = turn(bank[7][:, P * c:P * c + P], vT[:, tok(c)])
                last.then_inc(vn_tr, 1)
                turn(bank[5][0:NS, 0:P], vT[:, T:NT]).then_inc(vn_tr, 1)
                pe.wait_ge(rot_done, 2 * h + 2)
                if h:
                    pe.wait_ge(rn_mix, h)
                for c in range(4):
                    last = mm(bank[6][:, P * c:P * c + P], kq[:, 0, tok(c)], kq[:, 1, tok(c)], start=True, stop=True)
                last.then_inc(sT_mm, 1)
                pe.wait_ge(vn_ev, h + 1)
                for c in range(4):
                    last = mm(bank[4][:, P * c:P * c + P], kn[:, c, :], vn[:, c, :], start=True, stop=True)
                last.then_inc(u_mm, 1)
                pe.wait_ge(vx_ready, h + 1)
                for j in range(2):
                    mm(bank[(5, 7)[j]][:, :], kns[:, :], vx[:, 4 * j:4 * j + 4, :].rearrange("p b e -> p (b e)"),
                       start=True, stop=True).then_inc(us_mm, 1)
            outputs(NH - 1)

            def sample_norm():
                pe.wait_ge(os_ev, NH)
                turn(bank[7][0:64, 0:P], OS[:, :, :].rearrange("p h b -> p (h b)")).then_inc(gs_tr, 1)
                turn_outputs(NH - 1)

            def turn_y(k, which=range(3), step=None):
                v = step or Known(k + NB_IN + 1)
                pe.wait_ge(acc_free, v(4, -2 if which == (0,) else 0))
                if k:
                    pe.wait_ge(y_add, v(3, -3 * (NB_IN + 1)))
                for j in which:
                    if j < 2:
                        for t in range(2):
                            for m in range(2):
                                last = turn(bank[4 + j][:, 256 * t + P * m:256 * t + P * m + P], yT[:, m, tok(2 * j + t)])
                    else:
                        for m in range(2):
                            last = turn(bank[6][0:NS, P * m:P * m + P], yT[:, m, T:NT])
                    last.then_inc(y_tr, 1)

            chunk(NB_IN, 0, sample_norm)
            pe.wait_ge(gs_n, 1)
            turn(bank[7][:, 0:64], nrm[0:64, 0, :], 64).then_inc(gs_tr, 1)
            chunk(NB_IN, 1)
            chunk(NB_IN + 1, 0)
            turn_y(0)
            chunk(NB_IN + 1, 1)
            with pe.Fori(NB_IN + 2, NB - 1) as n:
                m = NB_IN + 2
                step = Step(pe, n, (2, 1), (2, 2), (4, -3), (4, -2), (4, -1), (4, 0), (3, -3 * (NB_IN + 1)))
                chunk(m, 0, step=step)
                turn_y(1, step=step)
                chunk(m, 1, step=step)
            n = NB - 1
            pe.wait_ge(w_lo, 2 * n + 1)
            part(n, 0, 0)
            part(n, 0, 2)
            turn_y(6)
            part(n, 0, 1)
            pe.wait_ge(w_lo, 2 * n + 2)
            part(n, 1, 0)
            part(n, 1, 2)
            part(n, 1, 1)
            turn_y(7, (0,))
            part(n, 0, 3)
            part(n, 1, 3)
            turn_y(7, (1, 2))


def _tables():
    import numpy as np
    half = 64
    inv = np.float32(10000.0) ** (-np.arange(half, dtype=np.float32) / np.float32(half))
    pos = np.concatenate([np.arange(512), np.full(8, 4096)]).astype(np.float32)
    ang = (inv[:, None].astype(np.float32) * pos[None, :]).astype(np.float32).astype(np.float64)
    rot = np.zeros((128, 2, 520), np.float32)
    rot[0:64, 0] = rot[64:128, 0] = np.cos(ang)
    rot[0:64, 1] = -np.sin(ang)
    rot[64:128, 1] = np.sin(ang)
    j = np.arange(128, dtype=np.float64)
    tri = (j[None, :] >= j[:, None]).astype(np.float32)
    bias = np.where(j[None, :] <= j[:, None], 0.0, -1e30).astype(np.float32)
    cols = np.zeros((128, 8, 8), np.float32)
    cols[:, 7] = j[:, None] // 16 == np.arange(8)
    cols[0:24, 6, 0] = -1e38
    cols[0:8, 6, 1] = 1024.0 * j[0:8]
    for h in range(8):
        lg = np.log1p(-2.0 ** (-5.0 - h))
        cols[:, 0, h] = 128.0 ** -0.5 * np.exp(-(j + 1) * lg)
        cols[:, 1, h] = 128.0 ** -0.5 * np.exp((127 - j) * lg)
        cols[:, 2, h] = np.exp((j + 1) * lg)
        cols[:, 3, h] = np.exp(2 * (j + 1) * lg)
        cols[:, 4, h] = np.exp(128 * lg)
        cols[:, 5, h] = j % 16
    return {"c_ident": np.eye(128, dtype=np.float32), "c_rot": rot, "c_tri": tri, "c_bias": bias, "c_cols": cols,
            "c_eye": np.eye(8, dtype=np.float32)}


_INS = ["x_prompt", "x_sample", "cache_k", "cache_v", "cache_kidx", "state_ret", "page_table", "norm_g", "w_in",
        "ret_norm_g", "w_out", "final_norm_g"]
_OUTS = [(1, 512, 2048), (8, 1, 2048), (1, 1, 512, 2, 128), (1, 1, 512, 2, 128), (1, 1, 512, 128),
         (1, 1, 8, 128, 128), (1, 8, 1, 2, 128), (1, 8, 1, 2, 128), (1, 8, 1, 128), (1, 8, 8, 128, 128)]


def kernel(**inputs):
    import numpy as np
    import concourse.bacc as bacc
    from concourse.bass_utils import run_bass_kernel_spmd

    nc = bacc.Bacc("TRN2", target_bir_lowering=False, num_devices=1)
    arrays, args = {}, []
    given = {name: np.ascontiguousarray(inputs[name]) for name in _INS}
    given.update(_tables())
    for name, a in given.items():
        arrays[f"in_{name}"] = a
        args.append(nc.dram_tensor(f"in_{name}", a.shape, mybir.dt.from_np(a.dtype), kind="ExternalInput").ap())
    for i, shape in enumerate(_OUTS):
        args.append(nc.dram_tensor(f"out_{i}", shape, F32, kind="ExternalOutput").ap())
    build(nc, *args)
    r = run_bass_kernel_spmd(nc, [arrays], core_ids=[0])
    return tuple(r.results[0][f"out_{i}"] for i in range(len(_OUTS)))
```
